# Optimizing a Trainium2 kernel written in Bass

```python
import math
import jax, jax.numpy as jnp
from jax import lax
import numpy as np

D_MODEL = 1024
BATCH = 1
SEQ = 512
DEPTH = 1

D_MIX = D_MODEL
POOL_WIDTH = D_MIX // 4
POOL_WINDOWS = (2, 4, 8, 16)
POOL_GROUP = POOL_WIDTH // len(POOL_WINDOWS)
ATT_WIDTH = D_MIX - POOL_WIDTH
HEAD_DIM = 64
N_ATT_HEADS = ATT_WIDTH // HEAD_DIM
DILATED_GROUPS = ((128, 1), (512, 4), (2048, 16))
ATT_BLOCK = 128
N_BUCKETS = 32
MAX_DISTANCE = 2048
N_EXPERTS = 32
TOP_K = 4
D_FF = D_MODEL
SWIGLU_LIMIT = 7.0
SWIGLU_ALPHA = 1.702
MOE_BLOCK = 128
RMS_EPS = 1e-5
NEG_INF = -1e30

kernel_name = 'hybrid_pool_dilated_attn_moe'

def rmsnorm(x, g):
    xf = x.astype(jnp.float32)
    y = xf * lax.rsqrt(jnp.mean(xf * xf, axis=-1, keepdims=True) + RMS_EPS)
    return (y * g.astype(jnp.float32)).astype(x.dtype)

def pool_mixer(u, pool_w, pool_scale):
    B, S, _ = u.shape
    maxw = max(POOL_WINDOWS)
    uf = u.astype(jnp.float32)
    c = jnp.cumsum(uf, axis=1)
    c_pad = jnp.pad(c, ((0, 0), (maxw, 0), (0, 0)))
    t = jnp.arange(S)
    outs = []
    for g, w in enumerate(POOL_WINDOWS):
        lo, hi = g * POOL_GROUP, (g + 1) * POOL_GROUP
        win_sum = c_pad[:, maxw:, lo:hi] - c_pad[:, maxw - w:maxw - w + S, lo:hi]
        cnt = jnp.minimum(t + 1, w).astype(jnp.float32)[None, :, None]
        outs.append(win_sum / cnt - uf[:, :, lo:hi])
    pooled = jnp.stack(outs, axis=2).astype(u.dtype)
    mixed = jnp.einsum('bsgc,gcd->bsgd', pooled, pool_w)
    return mixed.reshape(B, S, POOL_WIDTH) * pool_scale

def t5_bucket(dist):
    max_exact = N_BUCKETS // 2
    is_small = dist < max_exact
    nf = jnp.maximum(dist, 1).astype(jnp.float32)
    large = max_exact + (jnp.log(nf / max_exact) / math.log(MAX_DISTANCE / max_exact)
                         * (N_BUCKETS - max_exact)).astype(jnp.int32)
    large = jnp.minimum(large, N_BUCKETS - 1)
    return jnp.where(is_small, dist, large)

def dilated_branch(q, k, v, rel_bias, window, dil):
    B, S, H, Dh = q.shape
    w_sub = window // dil
    assert w_sub <= ATT_BLOCK
    span = dil * ATT_BLOCK
    S_pad = -(-S // span) * span
    M = S_pad // dil
    nb = M // ATT_BLOCK

    def to_blocks(a):
        a = jnp.pad(a, ((0, 0), (0, S_pad - S), (0, 0), (0, 0)))
        a = a.reshape(B, M, dil, H, Dh).transpose(0, 2, 1, 3, 4)
        return a.reshape(B, dil, nb, ATT_BLOCK, H, Dh)

    def band(a):
        prev = jnp.pad(a[:, :, :-1], ((0, 0), (0, 0), (1, 0), (0, 0), (0, 0), (0, 0)))
        return jnp.concatenate([prev, a], axis=3)

    qb = to_blocks(q)
    kb = band(to_blocks(k))
    vb = band(to_blocks(v))

    qi = jnp.arange(ATT_BLOCK)[:, None]
    kj = jnp.arange(2 * ATT_BLOCK)[None, :]
    dist = qi + ATT_BLOCK - kj
    in_win = (dist >= 0) & (dist <= w_sub)
    bias = rel_bias[t5_bucket(jnp.clip(dist, 0) * dil)]
    bias = bias.transpose(2, 0, 1).astype(jnp.float32)
    has_prev = (jnp.arange(nb)[:, None, None] > 0) | (kj >= ATT_BLOCK)[None]
    mask = in_win[None] & has_prev

    s = jnp.einsum('brnqhd,brnkhd->brnhqk', qb, kb).astype(jnp.float32) * (HEAD_DIM ** -0.5)
    s = jnp.where(mask[None, None, :, None], s + bias[None, None, None], NEG_INF)
    m = jnp.max(s, axis=-1, keepdims=True)
    p = jnp.exp(s - m)
    l = jnp.sum(p, axis=-1, keepdims=True)
    o = jnp.einsum('brnhqk,brnkhd->brnqhd', (p / l).astype(v.dtype), vb)
    lse = (m + jnp.log(l))[..., 0]

    o = o.reshape(B, dil, M, H, Dh).transpose(0, 2, 1, 3, 4).reshape(B, S_pad, H, Dh)[:, :S]
    lse = lse.transpose(0, 1, 2, 4, 3).reshape(B, dil, M, H).transpose(0, 2, 1, 3)
    lse = lse.reshape(B, S_pad, H)[:, :S]
    return o, lse

def dilated_attention(q, k, v, rel_bias):
    outs, lses = [], []
    for window, dil in DILATED_GROUPS:
        o, lse = dilated_branch(q, k, v, rel_bias, window, dil)
        outs.append(o)
        lses.append(lse)
    wts = jax.nn.softmax(jnp.stack(lses, axis=0), axis=0)
    o = jnp.stack(outs, axis=0).astype(jnp.float32)
    return jnp.sum(wts[..., None] * o, axis=0).astype(q.dtype)

def clamped_swiglu(gu):
    gate, up = gu[..., :D_FF], gu[..., D_FF:]
    gate = jnp.minimum(gate, SWIGLU_LIMIT)
    up = jnp.clip(up, -SWIGLU_LIMIT, SWIGLU_LIMIT)
    return (up + 1.0) * (gate * jax.nn.sigmoid(gate * SWIGLU_ALPHA))

def moe(h, router_w, router_b, w_gate_up, b_gate_up, w_down, b_down):
    N, D = h.shape
    logits = (h @ router_w + router_b).astype(jnp.float32)
    top_v, top_i = lax.top_k(logits, TOP_K)
    gates = jax.nn.softmax(top_v, axis=-1)
    A = N * TOP_K
    e_flat = top_i.reshape(A)
    g_flat = gates.reshape(A)
    tok_flat = jnp.arange(A, dtype=jnp.int32) // TOP_K
    order = jnp.argsort(e_flat)
    e_s, tok_s, g_s = e_flat[order], tok_flat[order], g_flat[order]
    counts = jnp.zeros((N_EXPERTS,), jnp.int32).at[e_flat].add(1)
    starts = jnp.cumsum(counts) - counts
    blocks_per = (counts + MOE_BLOCK - 1) // MOE_BLOCK
    block_end = jnp.cumsum(blocks_per)
    pstarts = (block_end - blocks_per) * MOE_BLOCK
    dest = pstarts[e_s] + (jnp.arange(A, dtype=jnp.int32) - starts[e_s])
    nb = -(-A // MOE_BLOCK) + N_EXPERTS
    P = nb * MOE_BLOCK
    slot_tok = jnp.full((P,), N, jnp.int32).at[dest].set(tok_s)
    slot_gate = jnp.zeros((P,), h.dtype).at[dest].set(g_s.astype(h.dtype))
    block_exp = jnp.minimum(jnp.searchsorted(block_end, jnp.arange(nb, dtype=jnp.int32), side='right'),
                            N_EXPERTS - 1)
    h_pad = jnp.concatenate([h, jnp.zeros((1, D), h.dtype)], axis=0)
    xb = h_pad[slot_tok].reshape(nb, MOE_BLOCK, D)

    def expert_block(args):
        xblk, e = args
        act = clamped_swiglu(xblk @ w_gate_up[e] + b_gate_up[e])
        return act @ w_down[e] + b_down[e]

    yb = lax.map(expert_block, (xb, block_exp)).reshape(P, D)
    out = jnp.zeros((N + 1, D), h.dtype).at[slot_tok].add(yb * slot_gate[:, None])
    return out[:N]

def setup_inputs(seed: int = 0) -> dict:
    key = jax.random.key(seed)
    ks = jax.random.split(key, 16)
    f32 = jnp.float32
    n_in = POOL_WIDTH + 3 * ATT_WIDTH
    nrm = lambda k, shape, scale: jax.random.normal(k, shape, f32) * scale
    return {
        'x': jax.random.normal(ks[0], (BATCH, SEQ, D_MODEL), f32),
        'norm1_g': 1.0 + nrm(ks[1], (DEPTH, D_MODEL), 0.05),
        'w_in': nrm(ks[2], (DEPTH, D_MODEL, n_in), D_MODEL ** -0.5),
        'pool_w': nrm(ks[3], (DEPTH, len(POOL_WINDOWS), POOL_GROUP, POOL_GROUP), POOL_GROUP ** -0.5),
        'pool_scale': 1.0 + nrm(ks[4], (DEPTH, POOL_WIDTH), 0.1),
        'rel_bias': nrm(ks[5], (N_BUCKETS, N_ATT_HEADS), 0.5),
        'w_out': nrm(ks[6], (DEPTH, D_MIX, D_MODEL), D_MIX ** -0.5),
        'norm2_g': 1.0 + nrm(ks[7], (DEPTH, D_MODEL), 0.05),
        'router_w': nrm(ks[8], (DEPTH, D_MODEL, N_EXPERTS), D_MODEL ** -0.5),
        'router_b': nrm(ks[9], (DEPTH, N_EXPERTS), 0.01),
        'w_gate_up': nrm(ks[10], (DEPTH, N_EXPERTS, D_MODEL, 2 * D_FF), D_MODEL ** -0.5),
        'b_gate_up': nrm(ks[11], (DEPTH, N_EXPERTS, 2 * D_FF), 0.02),
        'w_down': nrm(ks[12], (DEPTH, N_EXPERTS, D_FF, D_MODEL), D_FF ** -0.5),
        'b_down': nrm(ks[13], (DEPTH, N_EXPERTS, D_MODEL), 0.02),
        'final_g': 1.0 + nrm(ks[14], (D_MODEL,), 0.05),
    }

def reference(x, norm1_g, w_in, pool_w, pool_scale, rel_bias, w_out, norm2_g,
              router_w, router_b, w_gate_up, b_gate_up, w_down, b_down, final_g):
    B, S, D = x.shape
    for l in range(DEPTH):
        h = rmsnorm(x, norm1_g[l])
        proj = h @ w_in[l]
        u = proj[..., :POOL_WIDTH]
        qkv = proj[..., POOL_WIDTH:].reshape(B, S, 3, N_ATT_HEADS, HEAD_DIM)
        q, k, v = qkv[:, :, 0], qkv[:, :, 1], qkv[:, :, 2]
        pool_out = pool_mixer(u, pool_w[l], pool_scale[l])
        att_out = dilated_attention(q, k, v, rel_bias).reshape(B, S, ATT_WIDTH)
        mix = jnp.concatenate([pool_out.astype(x.dtype), att_out], axis=-1)
        x = x + mix @ w_out[l]
        h2 = rmsnorm(x, norm2_g[l]).reshape(B * S, D)
        x = x + moe(h2, router_w[l], router_b[l], w_gate_up[l], b_gate_up[l],
                    w_down[l], b_down[l]).reshape(B, S, D)
    return rmsnorm(x, final_g)


_drawn_inputs = setup_inputs


def setup_inputs(seed=0):
    import zlib

    import numpy as np

    out = dict(_drawn_inputs(seed))
    spreads = {}
    factors = {'b_gate_up': 5.538, 'b_down': 6.299}
    for name, (base, spread) in spreads.items():
        noise = np.random.default_rng([zlib.crc32(name.encode()), seed]).standard_normal(out[name].shape)
        drawn = base * np.exp(spread * noise) if base else spread * noise
        out[name] = __import__('jax').numpy.asarray(drawn.astype(out[name].dtype))
    for name, factor in factors.items():
        out[name] = (out[name] * factor).astype(out[name].dtype)
    return out
```

```python
import math
from contextlib import ExitStack

import concourse.bass as bass
import numpy as np
from concourse import mybir

F32 = mybir.dt.float32
F16 = mybir.dt.float16
I32 = mybir.dt.int32
U32 = mybir.dt.uint32
ALU = mybir.AluOpType
ACT = mybir.ActivationFunctionType
AX = mybir.AxisListType

P = 128
D = 1024
S = 512
TT = S // P
KT = D // P
POOL_W = 256
WINDOWS = (2, 4, 8, 16)
PG = POOL_W // 4
HEADS = 12
DH = 64
PAIRS = HEADS // 2
ATT_W = HEADS * DH
BUCKETS = 32
MAX_DIST = 2048
BRANCHES = ((128, 1), (512, 4), (2048, 16))
E = 32
TOPK = 4
FF = 1024
EPS = 1e-5
LIMIT = 7.0
ALPHA = 1.702
MASKED = -1e30

CH = 32
NCH = P // CH
Q = D // 4
UNIT = 2048
RING = 12
IN_UNITS = 10
OUT_UNITS = 4
PRE = IN_UNITS + OUT_UNITS
JOB_UNITS = 12
FREED = JOB_UNITS - 2
JOBS_MAX = 48
FAR = 4096
SKIP = 16384
RLEN = 640

C_ID, C_TRI, C_ONE = 0, 128, 256
C_IOTA = 384
C_TOK = 416
C_CNT = 432
C_INVW = 464
C_SKIPJ = 466
C_PART = 467
C_TOK4 = 468
C_END = 472


def bucket_of(dist):
    exact = BUCKETS // 2
    nf = np.maximum(dist, 1).astype(np.float32)
    large = exact + (np.log(nf / np.float32(exact)) / np.float32(math.log(MAX_DIST / exact))
                     * np.float32(BUCKETS - exact)).astype(np.int32)
    return np.where(dist < exact, dist, np.minimum(large, BUCKETS - 1))


def constants():
    c = np.zeros((P, C_END), np.float32)
    p = np.arange(P)
    c[:, C_ID:C_ID + P] = np.eye(P)
    c[:, C_TRI:C_TRI + P] = p[:, None] < p[None, :]
    c[:, C_ONE:C_ONE + P] = 1.0
    c[:, C_IOTA:C_IOTA + E] = np.arange(E)
    tok = np.arange(TT)[None, :] * P + p[:, None]
    c[:, C_TOK:C_TOK + TT * TOPK] = (16 * tok[:, :, None] + 4 * np.arange(TOPK)).reshape(P, -1)
    for m in range(2):
        w = np.where(p < PG, WINDOWS[2 * m], WINDOWS[2 * m + 1]).astype(np.float32)
        cnt = np.minimum(np.arange(16)[None, :] + 1, w[:, None]).astype(np.float32)
        c[:, C_CNT + 16 * m:C_CNT + 16 * (m + 1)] = w[:, None] / cnt
        c[:, C_INVW + m] = 1.0 / w
    c[:, C_SKIPJ] = SKIP + p // CH
    c[:, C_PART] = p
    c[:, C_TOK4:C_TOK4 + TT] = 4 * tok
    dist = np.arange(RLEN) - (P - 1)
    count = sum(((dist % dil == 0) & (dist <= window)).astype(np.float64) for window, dil in BRANCHES)
    seen = (dist >= 0) & (count > 0)
    sel = np.zeros((BUCKETS + 1, RLEN), np.float32)
    sel[bucket_of(np.maximum(dist, 0))[seen], np.arange(RLEN)[seen]] = 1.0
    sel[BUCKETS] = np.where(seen, np.log(np.maximum(count, 1)), MASKED)
    return c, sel


def tri(i):
    return i * (i + 1) // 2


def program(nc, x, w_in, w_out, norm1, norm2, final_g, rel_bias, pool_w, pool_scale, router_w,
            router_b, w_gate_up, w_down, biases, consts, selector, out):
    xv = x.rearrange("(t p) d -> t p d", p=P)
    outv = out.rearrange("(t p) d -> t p d", p=P)
    bias_by_dist = nc.dram_tensor("bias_by_dist", [HEADS, RLEN], F32).ap()
    h2_rows = nc.dram_tensor("h2_rows", [S * 4, Q], F32).ap()
    y_rows = nc.dram_tensor("y_rows", [S * TOPK * 4, Q], F32).ap()

    with ExitStack() as ctx:
        def sb(name, shape, dt=F32):
            return ctx.enter_context(nc.sbuf_tensor(name, shape, dt))

        def sem(name):
            return ctx.enter_context(nc.semaphore(name))

        bank = [ctx.enter_context(nc.psum_tensor(f"bank{i}", [P, 512], F32)) for i in range(8)]

        ring = sb("ring", [P, RING, UNIT])
        xs = sb("xs", [P, TT, D])
        hT = sb("hT", [P, KT, S])
        mixr = sb("mixr", [P, KT * S + 64])
        mixT = mixr[:, 0:KT * S].rearrange("p (k s) -> p k s", k=KT)
        gain = sb("gain", [P, D])
        cst = sb("cst", [P, C_END])
        rw = sb("rw", [P, KT, E])
        bias_all = sb("bias_all", [P, 3 * Q])
        rb = sb("rb", [1, E])
        relb = sb("relb", [BUCKETS + 1, HEADS])
        pw = sb("pw", [P, 2, PG])
        pscale = sb("pscale", [P, 2])
        work = sb("work", [P, 12288])

        ident = cst[:, C_ID:C_ID + P]
        tri_c = cst[:, C_TRI:C_TRI + P]
        ones = cst[:, C_ONE:C_ONE + P]

        st = sb("st", [P, 96])
        ssq, rstd = st[:, 0:4], st[:, 4:8]
        neg_max, row_sum, row_inv = st[:, 8:10], st[:, 10:12], st[:, 12:14]
        row_max = st[:, 14:16]
        eps = st[:, 16:17]
        gates, gsum, ginv = st[:, 20:36], st[:, 36:40], st[:, 40:44]
        job_r, job_p, keep_s = st[:, 44:48], st[:, 48:52], st[:, 52:56]

        qk = work[:, 0:2048].rearrange("p (b w s) -> p b w s", b=2, w=2)
        v = work[:, 2048:5120].rearrange("p (t c) -> p t c", t=TT)
        prob = work[:, 5120:7680].rearrange("p (h n) -> p h n", h=2)
        probT = work[:, 7680:10240].rearrange("p (h n) -> p h n", h=2)
        btab = work[:, 10240:12288].rearrange("p (b h n) -> p b h n", b=2, h=2)
        hbuf = work[:, 5120:7168].rearrange("p (b d) -> p b d", b=2)
        sq_junk = work[:, 7680:8704]
        r_sb = work[0:HEADS, 8704:8704 + RLEN]
        sel_sb = work[0:BUCKETS + 1, 9344:9344 + RLEN]
        pa = mixr[:, 1024:1024 + 1040].rearrange("p (m s) -> p m s", m=2)
        pb = mixr[:, 2064:2064 + 1040].rearrange("p (m s) -> p m s", m=2)
        pc = mixr[:, 3104:3104 + 1040].rearrange("p (m s) -> p m s", m=2)

        o = 8704
        logits = work[:, o:o + 128].rearrange("p (t e) -> p t e", t=TT)
        top = work[:, o + 128:o + 160].rearrange("p (t k) -> p t k", t=TT)
        topi = work[:, o + 160:o + 192].bitcast(U32).rearrange("p (t k) -> p t k", t=TT)
        topf = work[:, o + 192:o + 224].rearrange("p (t k) -> p t k", t=TT)
        chose = work[:, o + 224:o + 736].rearrange("p (t k e) -> p t k e", t=TT, k=TOPK)
        mask = work[:, o + 736:o + 864].rearrange("p (t e) -> p t e", t=TT)
        rank = work[:, o + 864:o + 992].rearrange("p (t e) -> p t e", t=TT)
        pos4 = work[:, o + 992:o + 1120].rearrange("p (t e) -> p t e", t=TT)
        cnt = work[:, o + 1120:o + 1152]
        nblk = work[:, o + 1152:o + 1184]
        tmp32 = work[:, o + 1184:o + 1216]
        blk_end = work[:, o + 1216:o + 1248]
        before = work[:, o + 1248:o + 1280]
        jcol = work[:, o + 1280:o + 1296]
        jdiag = work[:, o + 1296:o + 1296 + 3 * JOBS_MAX]
        o2 = o + 1296 + 3 * JOBS_MAX
        jobs_f = sb("jobs_f", [P, 3, JOBS_MAX])
        jobs_i = sb("jobs_i", [P, 3, JOBS_MAX], I32)
        njobs_i = sb("njobs_i", [P, 1], I32)
        ahead = sb("ahead", [16, NCH, 4])

        gu = work[:, 0:1024].rearrange("p (b n) -> p b n", b=2)
        sg = work[:, 1024:1536].rearrange("p (b n) -> p b n", b=2)
        act_q = work[:, 1536:2048].rearrange("p (b n) -> p b n", b=2)
        yb = work[:, 2048:3072].rearrange("p (c n) -> p c n", c=NCH)
        bt = work[:, 3072:3840]
        pick = work[:, 3840:3968]
        hot = work[:, 10240:11264].bitcast(F16).rearrange("p (t n) -> p t n", t=TT)
        slot = work[:, 11264:11520].bitcast(F16)
        pcol = work[:, 11520:11528].bitcast(F16)[:, 0:3 * TT].rearrange("p (t n) -> p t n", t=TT)
        idx_t = work[:, 11536:11544].rearrange("p (c n) -> p c n", c=NCH)
        idx_g = work[:, 11552:11556].bitcast(U32)
        idx_s = work[:, 11560:11568].bitcast(U32).rearrange("p (b c) -> p b c", b=2)
        xg = hT[:, 0:2, :].rearrange("p a (c n) -> p (a c) n", c=2)
        xT = hT[:, 2:4, :].rearrange("p a (c n) -> p (a c) n", c=2)
        aT = hT[:, 4:6, :].rearrange("p a (c n) -> p (a c) n", c=2)

        cst_in, small_in, gain_in = sem("cst_in"), sem("small_in"), sem("gain_in")
        x_in = [sem(f"x_in{t}") for t in range(TT)]
        slot_full = [sem(f"slot_full{s}") for s in range(RING)]
        units_used = sem("units_used")
        eps_set = sem("eps_set")
        ssq_done = sem("ssq_done")
        sqrt_done = sem("sqrt_done")
        rstd_done = sem("rstd_done")
        h_done = sem("h_done")
        tr_done = sem("tr_done")
        tr_act = sem("tr_act")
        tr_dve = sem("tr_dve")
        relb_one = sem("relb_one")
        r_mm, r_copied, r_out = sem("r_mm"), sem("r_copied"), sem("r_out")
        bt_in = [sem(f"bt_in{b}") for b in range(2)]
        proj_done = sem("proj_done")
        proj_act = sem("proj_act")
        u_pad = sem("u_pad")
        pool_step = sem("pool_step")
        pooled = sem("pooled")
        poolmm = sem("poolmm")
        pool_out = sem("pool_out")
        score_done = sem("score_done")
        score_read = sem("score_read")
        negmax_done = sem("negmax_done")
        exp_done = sem("exp_done")
        inv_done = sem("inv_done")
        norm_done = sem("norm_done")
        pt_done = sem("pt_done")
        pt_dve, pt_act = sem("pt_dve"), sem("pt_act")
        pv_done = sem("pv_done")
        att_out = sem("att_out")
        op_done = sem("op_done")
        x2_half, x2_done = sem("x2_half"), sem("x2_done")
        h2_out = [sem(f"h2_out{b}") for b in range(2)]
        lg_done, lg_copied = sem("lg_done"), sem("lg_copied")
        step = sem("step")
        mask_done = sem("mask_done")
        rank_mm, cnt_mm = sem("rank_mm"), sem("cnt_mm")
        jdiag_done, jobs_mm, jobs_done = sem("jdiag_done"), sem("jobs_mm"), sem("jobs_done")
        gate_in, gate_exp, gate_done = sem("gate_in"), sem("gate_exp"), sem("gate_done")
        slot_set, xg_zero = sem("slot_set"), sem("xg_zero")
        hot_done = sem("hot_done")
        pick_done = sem("pick_done")
        idx_mm = sem("idx_mm")
        idx_done = sem("idx_done")
        gathered = [sem(f"gathered{c}") for c in range(NCH)]
        x_tr, x_copied = sem("x_tr"), sem("x_copied")
        bias_mm, bias_copied = sem("bias_mm"), sem("bias_copied")
        gu_done = sem("gu_done")
        gu_read = sem("gu_read")
        gate_clamped, sig_done, act_done = sem("gate_clamped"), sem("sig_done"), sem("act_done")
        t_done, t_copied = sem("t_done"), sem("t_copied")
        dn_done, y_done = sem("dn_done"), sem("y_done")
        scattered = [sem(f"scattered{c}") for c in range(NCH)]
        y_in = [sem(f"y_in{t}") for t in range(TT)]
        sum_done, fin_done, out_done = sem("sum_done"), sem("fin_done"), sem("out_done")
        pstep = sem("pstep")
        waited_sp, waited_pool = sem("waited_sp"), sem("waited_pool")

        def unit_slot(u):
            return (PRE + u) % RING

        def unit_loads(u):
            return PRE // RING + (1 if unit_slot(u) < PRE % RING else 0)

        def unit_full(u, job):
            return (unit_loads(u) + 1) * 16 + job * 16

        block = ctx.enter_context(nc.Block())

        @block.sync
        def _(sp):
            sp.dma_start(cst[:, :], consts).then_inc(cst_in, 16)
            for t in range(TT):
                sp.dma_start(xs[:, t, :], xv[t]).then_inc(x_in[t], 16)
            for n in range(PRE):
                if n >= RING:
                    sp.wait_ge(proj_done, 2 * (n - RING + 1))
                s = n % RING
                if n < IN_UNITS:
                    src = w_in[n]
                else:
                    a = (n - IN_UNITS) * 2 * P
                    src = w_out[a:a + 2 * P, :].rearrange("(k p) n -> p k n", p=P)
                dst = ring[:, s, :] if n < IN_UNITS else ring[:, s, :].rearrange("p (k n) -> p k n", k=2)
                sp.dma_start(dst, src).then_inc(slot_full[s], 16)

            def load_job(e, job, first):
                for u in range(JOB_UNITS):
                    if first and u < IN_UNITS - 2:
                        sp.wait_ge(proj_done, 2 * (PRE - RING + u + 1))
                    elif first:
                        sp.wait_ge(op_done, TT)
                    elif u == KT - 1:
                        sp.wait_ge(gu_done, job * NCH)
                    elif u == JOB_UNITS - 1:
                        sp.wait_ge(dn_done, job * NCH)
                    else:
                        sp.wait_ge(units_used, job * FREED + (u + 1 - (u >= KT) - FREED))
                    if not first:
                        sp.sem_inc(waited_sp, 1)
                    s = unit_slot(u)
                    if u < KT:
                        src = w_gate_up[bass.ds(e, 1), u * P:(u + 1) * P, :].rearrange("e p n -> p (e n)")
                        dst = ring[:, s, :]
                    else:
                        a = (u - KT) * 2 * P
                        src = w_down[bass.ds(e, 1), a:a + 2 * P, :].rearrange("e (k p) n -> p (e k) n", p=P)
                        dst = ring[:, s, :].rearrange("p (k n) -> p k n", k=2)
                    sp.dma_start(dst, src).then_inc(slot_full[s], 16)

            load_job(0, 0, True)
            sp.wait_ge(jobs_done, 2)
            njobs = sp.value_load(njobs_i[0:1, 0:1], min_val=E, max_val=JOBS_MAX - 1)
            all_out, all_down = sp.snap(njobs * 16 + 16), sp.snap(njobs * NCH)
            with sp.Fori(1, njobs) as job:
                e = sp.value_load(jobs_i[0:1, 0, bass.ds(job, 1)], min_val=0, max_val=E - 1)
                load_job(e, job, False)
            for c in range(NCH):
                sp.wait_ge(scattered[c], all_out)
                sp.sem_inc(waited_sp, 1)
            sp.wait_ge(dn_done, all_down)
            yv = y_rows.rearrange("(t p r) q -> t p (r q)", t=TT, p=P)
            for t in range(TT):
                sp.dma_start(ring[:, 3 * t:3 * t + 2, :].rearrange("p a n -> p (a n)"), yv[t]).then_inc(y_in[t], 16)
            for t in range(TT):
                sp.wait_ge(fin_done, t + 1)
                sp.dma_start(outv[t], ring[:, 3 * t + 2, 0:D]).then_inc(out_done, 16)
            sp.wait_ge(out_done, 16 * TT)

        @block.tensor
        def _(pe):
            pe.sem_inc(t_done, 1)
            pe.wait_ge(small_in, 16 * 7)
            pe.wait_ge(relb_one, 1)
            for a in range(2):
                mm = pe.matmul(bank[a][0:HEADS, 0:RLEN // 2], relb[:, :], sel_sb[:, a * RLEN // 2:(a + 1) * RLEN // 2],
                               start=True, stop=True)
            mm.then_inc(r_mm, 1)

            pe.wait_ge(cst_in, 16)

            def transposes(src_of, t, first, groups):
                for g in range(2):
                    if groups >= 2:
                        pe.wait_ge(tr_act if g == 0 else tr_dve, groups // 2)
                    for k in range(4):
                        mm = pe.transpose(bank[4 + g][:, k * P:(k + 1) * P],
                                          src_of[:, (4 * g + k) * P:(4 * g + k + 1) * P], ident)
                    mm.then_inc(tr_done, 1)

            for t in range(TT):
                pe.wait_ge(h_done, t + 1)
                transposes(hbuf[:, t % 2, :], t, 0, 2 * t)
            pe.wait_ge(tr_act, TT)
            pe.wait_ge(tr_dve, TT)
            pe.wait_ge(r_copied, 2)

            groups = [0]

            def projection_bank():
                n = groups[0]
                groups[0] += 1
                if n >= 2:
                    pe.wait_ge(proj_act, n - 1)
                return bank[n % 2]

            def project_unit(unit):
                pe.wait_ge(slot_full[unit], 16)
                for half in range(2):
                    w = ring[:, unit, :].rearrange("p (k n) -> p k n", k=KT)
                    b = projection_bank()
                    for k in range(KT):
                        mm = pe.matmul(b[:, :], w[:, k, half * P:(half + 1) * P], hT[:, k, :],
                                       start=(k == 0), stop=(k == KT - 1))
                        if k == KT - 1:
                            mm.then_inc(proj_done, 1)
                        if k % 4 == 3:
                            yield

            def project_values(unit, i):
                pe.wait_ge(slot_full[unit], 16)
                w = ring[:, unit, :].rearrange("p (k n) -> p k n", k=KT)
                for tp in range(2):
                    b = projection_bank()
                    for half in range(2):
                        t = 2 * tp + half
                        for k in range(KT):
                            mm = pe.matmul(b[:, half * 256:(half + 1) * 256], hT[:, k, t * P:(t + 1) * P], w[:, k, :],
                                           start=(k == 0), stop=(k == KT - 1))
                    mm.then_inc(proj_done, 1)

            def scores(pr, i):
                n = TT * pr + i
                if n >= 1:
                    pe.wait_ge(score_read, n)
                for h in range(2):
                    r = slice(h * DH, (h + 1) * DH)
                    mm = pe.matmul(bank[2 + h][:, 0:(i + 1) * P], qk[r, pr % 2, 0, i * P:(i + 1) * P],
                                   qk[r, pr % 2, 1, 0:(i + 1) * P], start=True, stop=True)
                mm.then_inc(score_done, 1)

            def flip(pr, i):
                n = TT * pr + i
                pe.wait_ge(norm_done, 2 * (n + 1))
                if n >= 1:
                    pe.wait_ge(pt_dve, n)
                    pe.wait_ge(pt_act, n)
                for h in range(2):
                    for kb in range(i + 1):
                        a = (tri(i) + kb) * P
                        mm = pe.transpose(bank[4 + h][:, kb * P:(kb + 1) * P], prob[:, h, a:a + P], ident)
                mm.then_inc(pt_done, 1)

            def values(pr, i):
                n = TT * pr + i
                pe.wait_ge(pt_dve, n + 1)
                pe.wait_ge(pt_act, n + 1)
                if i == 0 and pr >= 1:
                    pe.wait_ge(att_out, pr)
                for kb in range(i + 1):
                    for h in range(2):
                        a = (tri(i) + kb) * P
                        c = (2 * pr + h) * DH
                        mm = pe.matmul(bank[6][h * DH:(h + 1) * DH, i * P:(i + 1) * P], v[:, kb, c:c + DH],
                                       probT[:, h, a:a + P], start=(kb == 0), stop=(kb == i))
                if i == TT - 1:
                    mm.then_inc(pv_done, 1)

            for _ in project_unit(0):
                pass
            for _ in project_unit(1):
                pass
            for i in range(3):
                project_values(2 + i, i)
            for it in range(PAIRS + 1):
                ahead = project_unit(5 + it) if it + 1 < PAIRS else None
                for i in range(TT):
                    if ahead is not None:
                        next(ahead)
                    if it >= 1:
                        flip(it - 1, i)
                    if it < PAIRS:
                        if i == 0:
                            pe.wait_ge(proj_act, 2 + 2 + 6 + 2 * it)
                        scores(it, i)
                    if it >= 1:
                        values(it - 1, i)
                if ahead is not None:
                    for _ in ahead:
                        pass
                if it == 0:
                    pe.wait_ge(pooled, 4)
                    for m in range(2):
                        if m:
                            pe.wait_ge(pool_out, 1)
                        for g in range(2):
                            r = slice(g * PG, (g + 1) * PG)
                            mm = pe.matmul(bank[7][r, :], pw[r, m, :], pa[r, m, 8:8 + S], start=True, stop=True)
                        mm.then_inc(poolmm, 1)

            def project_out(t):
                a = 2 * (t % 2)
                if t >= 2:
                    pe.wait_ge(x2_done, t - 1)
                for n in range(2):
                    for k in range(KT):
                        s = (IN_UNITS + k // 2) % RING
                        if t == 0 and n == 0 and k % 2 == 0:
                            pe.wait_ge(slot_full[s], 16 * ((IN_UNITS + k // 2) // RING + 1))
                        c = (k % 2) * D + n * 512
                        mm = pe.matmul(bank[a + n][:, :], mixT[:, k, t * P:(t + 1) * P], ring[:, s, c:c + 512],
                                       start=(k == 0), stop=(k == KT - 1))
                mm.then_inc(op_done, 1)

            def route(t):
                pe.wait_ge(h_done, TT + t + 1)
                transposes(hbuf[:, t % 2, :], t, TT, 2 * (TT + t))
                pe.wait_ge(tr_act, TT + t + 1)
                pe.wait_ge(tr_dve, TT + t + 1)
                if t >= 1:
                    pe.wait_ge(lg_copied, t)
                out_ = bank[6][:, t * E:(t + 1) * E]
                for k in range(KT):
                    pe.matmul(out_, hT[:, k, t * P:(t + 1) * P], rw[:, k, :], start=(k == 0), stop=False)
                pe.matmul(out_, ones[0:1, :], rb[:, :], start=False, stop=True).then_inc(lg_done, 1)

            pe.wait_ge(pool_out, 2)
            pe.wait_ge(att_out, PAIRS)
            pe.wait_ge(score_read, TT * PAIRS)
            pe.wait_ge(pt_dve, TT * PAIRS)
            pe.wait_ge(pt_act, TT * PAIRS)
            project_out(0)
            project_out(1)
            for t in range(TT):
                if t + 2 < TT:
                    route(t)
                    project_out(t + 2)
                else:
                    route(t)
            pe.wait_ge(mask_done, 1)
            for t in range(TT):
                for u in range(t + 1):
                    mm = pe.matmul(bank[0][:, t * E:(t + 1) * E], tri_c if u == t else ones, mask[:, u, :],
                                   start=(u == 0), stop=(u == t))
            mm.then_inc(rank_mm, 1)
            for t in range(TT):
                mm = pe.matmul(bank[1][:, 0:E], ones, mask[:, t, :], start=(t == 0), stop=(t == TT - 1))
            mm.then_inc(cnt_mm, 1)
            pe.wait_ge(jdiag_done, 1)
            pe.matmul(bank[1][:, 0:3 * JOBS_MAX], ones, jdiag, start=True, stop=True).then_inc(jobs_mm, 1)

            def indices(job):
                pe.wait_ge(hot_done, job + 1)
                for c in range(NCH):
                    for t in range(TT):
                        mm = pe.matmul(bank[7][:, 4 * c:4 * c + 3], hot[:, t, c * P:(c + 1) * P], pcol[:, t, :],
                                       start=(t == 0), stop=(t == TT - 1))
                mm.then_inc(idx_mm, 1)

            def flip_x(job, a):
                for c in (2 * a, 2 * a + 1):
                    pe.wait_ge(gathered[c], job * 16 + 16)
                if a == 1:
                    pe.wait_ge(x_copied, job * 2 + 1)
                for c in range(2):
                    for h in range(2):
                        mm = pe.transpose(bank[7][:, c * Q + h * P:c * Q + (h + 1) * P],
                                          xg[:, 2 * a + c, h * P:(h + 1) * P], ident)
                mm.then_inc(x_tr, 1)

            indices(0)
            pe.wait_ge(idx_done, 1)
            flip_x(0, 0)
            flip_x(0, 1)
            pe.wait_ge(jobs_done, 2)

            def run_job(job, m):
                def gate_up(c, k):
                    w = ring[:, unit_slot(k), :].rearrange("p (g n) -> p g n", g=2)
                    for j in range(4):
                        mm = pe.matmul(bank[c][j * CH:(j + 1) * CH, :].rearrange("p (g n) -> p g n", g=2),
                                       xT[:, c, (k % 2) * P + (k // 2) * CH:(k % 2) * P + (k // 2 + 1) * CH],
                                       w[:, :, j * Q:(j + 1) * Q], start=(k == 0), stop=(k == KT - 1),
                                       tile_position=(0, j * CH))
                    return mm

                for k in range(KT // 2):
                    pe.wait_ge(slot_full[unit_slot(k)], unit_full(k, job))
                    for c in range(m):
                        mm = gate_up(c, k)
                    mm.then_inc(units_used, 1)
                    if k == 0:
                        pe.wait_ge(pick_done, job + 1)
                        pe.matmul(bank[7][:, 0:2 * Q], pick, bias_all[:, 0:2 * Q], start=True, stop=True)\
                            .then_inc(bias_mm, 1)
                    if k == 1:
                        pe.wait_ge(bias_copied, job * 2 + 1)
                        pe.matmul(bank[7][:, 0:Q], pick, bias_all[:, 2 * Q:3 * Q], start=True, stop=True)\
                            .then_inc(bias_mm, 1)
                    if k == 2:
                        pe.wait_ge(bias_copied, job * 2 + 2)
                        indices(job + 1)
                for c in range(m):
                    for k in range(KT // 2, KT):
                        if c == 0:
                            pe.wait_ge(slot_full[unit_slot(k)], unit_full(k, job))
                        mm = gate_up(c, k)
                        if c == m - 1 and k < KT - 1:
                            mm.then_inc(units_used, 1)
                    mm.then_inc(gu_done, 1 if c < m - 1 else NCH - m + 1)

                def flip_act(c):
                    pe.wait_ge(act_done, job * NCH + (c + 1))
                    pe.wait_ge(t_copied, job * NCH + (c + 1))
                    for h in range(2):
                        mm = pe.transpose(bank[6][:, h * P:(h + 1) * P], act_q[:, c % 2, h * P:(h + 1) * P], ident)
                    mm.then_inc(t_done, 1 if c < m - 1 else NCH - m + 1)

                flip_act(0)
                pe.wait_ge(idx_done, job + 2)
                flip_x(job + 1, 0)
                pe.wait_ge(y_done, job * NCH + 1)
                for c in range(m):
                    if c + 1 < m:
                        flip_act(c + 1)
                    pe.wait_ge(t_copied, job * NCH + (c + 2))
                    if c >= 2:
                        pe.wait_ge(y_done, job * NCH + c)
                    for k in range(KT):
                        u = KT + k // 2
                        if c == 0 and k % 2 == 0:
                            pe.wait_ge(slot_full[unit_slot(u)], unit_full(u, job))
                        w = ring[:, unit_slot(u), (k % 2) * D:(k % 2 + 1) * D]
                        for j in range(4):
                            mm = pe.matmul(bank[4 + c % 2][j * CH:(j + 1) * CH, 0:Q],
                                           aT[:, c, (k % 2) * P + (k // 2) * CH:(k % 2) * P + (k // 2 + 1) * CH],
                                           w[:, j * Q:(j + 1) * Q], start=(k == 0), stop=(k == KT - 1),
                                           tile_position=(0, j * CH))
                        if c == m - 1 and k % 2 == 1 and k < KT - 1:
                            mm.then_inc(units_used, 1)
                    mm.then_inc(dn_done, 1 if c < m - 1 else NCH - m + 1)
                    if c == 0:
                        flip_x(job + 1, 1)

            njobs = pe.value_load(njobs_i[0:1, 0:1], min_val=E, max_val=JOBS_MAX - 1)
            with pe.Fori(0, njobs) as job:
                chunks = pe.value_load(jobs_i[0:1, 2, bass.ds(job, 1)], min_val=1, max_val=NCH)
                pe.wait_ge(x_copied, job * 2 + 2)
                pe.wait_ge(gu_read, job * NCH + 1)
                for m in range(1, NCH + 1):
                    with pe.If(chunks == m):
                        run_job(job, m)

        @block.scalar
        def _(act):
            act.sem_inc(t_copied, 1)
            for dst, src in ((relb[0:BUCKETS, :], rel_bias), (sel_sb, selector), (rw[:, :, :], router_w),
                             (bias_all[:, :], biases), (rb[:, :], router_b), (pw[:, :, :], pool_w),
                             (pscale[:, :], pool_scale)):
                act.dma_start(dst, src).then_inc(small_in, 16)
            act.dma_start(gain[:, :], norm1.partition_broadcast(P)).then_inc(gain_in, 16)
            act.wait_ge(eps_set, 1)

            def square(src, n):
                act.activation(sq_junk, src, ACT.Square, accum_out=ssq[:, n % TT:n % TT + 1]).then_inc(ssq_done, 1)

            def root(n, k):
                act.activation(rstd[:, n % TT:n % TT + k], ssq[:, n % TT:n % TT + k], ACT.Sqrt,
                               bias=eps, scale=1.0 / D).then_inc(sqrt_done, k)

            for t in range(TT):
                act.wait_ge(x_in[t], 16)
                if t:
                    act.wait_ge(ssq_done, t)
                square(xs[:, t, :], t)
            act.wait_ge(ssq_done, TT)
            root(0, TT)
            for t in range(TT):
                act.wait_ge(tr_done, 2 * t + 1)
                act.activation(hT[:, 0:4, t * P:(t + 1) * P], bank[4][:, :].rearrange("p (k s) -> p k s", k=4),
                               ACT.Copy).then_inc(tr_act, 1)
            act.wait_ge(h_done, TT)
            act.dma_start(gain[:, :], norm2.partition_broadcast(P)).then_inc(gain_in, 16)

            copies = [0]

            def copy_group(dst, width, scale=1.0):
                n = copies[0]
                copies[0] += 1
                act.wait_ge(proj_done, n + 1)
                src = bank[n % 2][:, :]
                if width:
                    src = src.rearrange("p (t c) -> p t c", c=width)
                act.activation(dst, src, ACT.Copy, scale=scale).then_inc(proj_act, 1)

            def copy_q(pr):
                copy_group(qk[:, pr % 2, 0, :], 0, DH ** -0.5)

            def copy_k(pr):
                copy_group(qk[:, pr % 2, 1, :], 0)

            act.wait_ge(u_pad, 1)
            for m in range(2):
                copy_group(pa[:, m, 8:8 + S], 0)
            copy_q(0)
            copy_k(0)
            for i in range(3):
                for tp in range(2):
                    copy_group(v[:, 2 * tp:2 * tp + 2, i * 256:(i + 1) * 256], 256)
            for it in range(PAIRS + 1):
                for i in range(TT):
                    if it + 1 < PAIRS and i == 1:
                        copy_q(it + 1)
                    if it + 1 < PAIRS and i == 3:
                        copy_k(it + 1)
                    if it >= 1:
                        n = TT * (it - 1) + i
                        act.wait_ge(pt_done, n + 1)
                        a = tri(i) * P
                        act.activation(probT[:, 1, a:a + (i + 1) * P], bank[5][:, 0:(i + 1) * P], ACT.Copy)\
                            .then_inc(pt_act, 1)
                    if it < PAIRS:
                        n = TT * it + i
                        act.wait_ge(negmax_done, n + 1)
                        a = tri(i) * P
                        for h in range(2):
                            pv = prob[:, h, a:a + (i + 1) * P]
                            act.activation(pv, pv, ACT.Exp, bias=neg_max[:, h:h + 1],
                                           accum_out=row_sum[:, h:h + 1]).then_inc(exp_done, 1)
                if it == 0:
                    for m in range(2):
                        act.wait_ge(poolmm, m + 1)
                        act.activation(mixT[:, m, :], bank[7][:, :], ACT.Copy, scale=pscale[:, m:m + 1])\
                            .then_inc(pool_out, 1)
                if it >= 1:
                    act.wait_ge(pv_done, it)
                    act.activation(mixT[:, 1 + it, :], bank[6][:, :], ACT.Copy).then_inc(att_out, 1)

            def copy_h2(t):
                act.wait_ge(tr_done, 2 * (TT + t) + 1)
                act.activation(hT[:, 0:4, t * P:(t + 1) * P], bank[4][:, :].rearrange("p (k s) -> p k s", k=4),
                               ACT.Copy).then_inc(tr_act, 1)

            for t in range(TT):
                act.wait_ge(x2_done, t + 1)
                act.wait_ge(ssq_done, TT + t)
                square(xs[:, t, :], TT + t)
                act.wait_ge(ssq_done, TT + t + 1)
                root(TT + t, 1)
                if t >= 1:
                    copy_h2(t - 1)
            copy_h2(TT - 1)
            act.wait_ge(h_done, 2 * TT)
            act.dma_start(gain[:, :], final_g.partition_broadcast(P)).then_inc(gain_in, 16)
            act.wait_ge(gate_in, 1)
            act.activation(gates, gates, ACT.Exp).then_inc(gate_exp, 1)

            def copy_x(job, a):
                act.wait_ge(x_tr, job * 2 + (a + 1))
                act.activation(xT[:, 2 * a:2 * a + 2, :], bank[7][:, :].rearrange("p (c n) -> p c n", c=2),
                               ACT.Copy).then_inc(x_copied, 1)

            copy_x(0, 0)
            copy_x(0, 1)
            act.wait_ge(jobs_done, 2)
            njobs = act.value_load(njobs_i[0:1, 0:1], min_val=E, max_val=JOBS_MAX - 1)
            with act.Fori(0, njobs) as job:
                act.wait_ge(y_done, job * NCH + 1)
                act.wait_ge(bias_mm, job * 2 + 1)
                act.activation(bt[:, 0:2 * Q], bank[7][:, 0:2 * Q], ACT.Copy).then_inc(bias_copied, 1)
                act.wait_ge(bias_mm, job * 2 + 2)
                act.activation(bt[:, 2 * Q:3 * Q], bank[7][:, 0:Q], ACT.Copy).then_inc(bias_copied, 1)

                def sigmoid(c):
                    act.wait_ge(gate_clamped, job * NCH + (c + 1))
                    act.activation(sg[:, c % 2, :], gu[:, c % 2, 0:Q], ACT.Sigmoid, scale=ALPHA)\
                        .then_inc(sig_done, 1)

                def copy_act(c):
                    act.wait_ge(t_done, job * NCH + (c + 2))
                    act.activation(aT[:, c, :], bank[6][:, 0:Q], ACT.Copy).then_inc(t_copied, 1)

                sigmoid(0)
                sigmoid(1)
                copy_act(0)
                copy_x(job + 1, 0)
                sigmoid(2)
                copy_act(1)
                copy_x(job + 1, 1)
                sigmoid(3)
                copy_act(2)
                copy_act(3)

            for t in range(TT):
                act.wait_ge(sum_done, t + 1)
                act.wait_ge(ssq_done, 2 * TT + t)
                square(xs[:, t, :], 2 * TT + t)
                act.wait_ge(ssq_done, 2 * TT + t + 1)
                root(2 * TT + t, 1)

        @block.gpsimd
        def _(pool):
            steps = [0]

            def link(ins):
                ins.then_inc(pstep, 1)
                steps[0] += 1
                pool.wait_ge(pstep, steps[0])

            for c in range(NCH):
                pool.dma_start(ahead[0:16, c, :], consts[0:16, 4 * c:4 * c + 4]).then_inc(scattered[c], 16)
            link(pool.memset(pb[:, :, 0:8], 0.0))
            link(pool.memset(pc[:, :, 0:8], 0.0))
            pool.memset(pa[:, :, 0:8], 0.0).then_inc(u_pad, 1)
            pool.wait_ge(r_copied, 2)
            pool.dma_start(bias_by_dist, r_sb).then_inc(r_out, 16)
            pool.wait_ge(r_out, 16)

            def load_table(pr):
                src = bass.AP(bias_by_dist.tensor, 2 * pr * RLEN, [[1, P], [RLEN, 2], [1, S]])
                pool.dma_start(btab[:, pr % 2, :, :], src).then_inc(bt_in[pr % 2], 16)

            load_table(0)
            load_table(1)
            pool.wait_ge(proj_act, 2)
            pool.wait_ge(u_pad, 1)
            pool.wait_ge(cst_in, 16)
            link(pool.tensor_tensor(pb[:, :, 8:8 + S], pa[:, :, 8:8 + S], pa[:, :, 7:7 + S], ALU.add))
            link(pool.tensor_tensor(pc[:, :, 8:8 + S], pb[:, :, 8:8 + S], pb[:, :, 6:6 + S], ALU.add))
            link(pool.tensor_tensor(pb[:, 1, 8:8 + S], pc[:, 1, 8:8 + S], pc[:, 1, 4:4 + S], ALU.add))
            link(pool.tensor_tensor(pc[PG:P, 1, 8:8 + S], pb[PG:P, 1, 8:8 + S], pb[PG:P, 1, 0:S], ALU.add))
            for m in range(2):
                for r, win in ((slice(0, PG), pb), (slice(PG, P), pc)):
                    ratio = cst[r, C_CNT + 16 * m:C_CNT + 16 * (m + 1)]
                    link(pool.tensor_tensor(win[r, m, 8:24], win[r, m, 8:24], ratio, ALU.mult))
                    link(pool.tensor_scalar(win[r, m, 8:8 + S], win[r, m, 8:8 + S],
                                            cst[r, C_INVW + m:C_INVW + m + 1], None, ALU.mult))
                    pool.tensor_tensor(pa[r, m, 8:8 + S], win[r, m, 8:8 + S], pa[r, m, 8:8 + S], ALU.subtract)\
                        .then_inc(pooled, 1)
            pool.wait_ge(pooled, 4)
            for pr in range(PAIRS):
                for i in range(TT):
                    n = TT * pr + i
                    pool.wait_ge(inv_done, n + 1)
                    a = tri(i) * P
                    for h in range(2):
                        pv = prob[:, h, a:a + (i + 1) * P]
                        pool.tensor_scalar(pv, pv, row_inv[:, h:h + 1], None, ALU.mult).then_inc(norm_done, 1)
                if pr + 2 < PAIRS:
                    pool.wait_ge(score_read, TT * (pr + 1))
                    load_table(pr + 2)
            h2v = h2_rows.rearrange("(t p r) q -> t p (r q)", t=TT, p=P)
            for t in range(TT):
                pool.wait_ge(h_done, TT + t + 1)
                pool.dma_start(h2v[t], hbuf[:, t % 2, :]).then_inc(h2_out[t % 2], 16)
            for b in range(2):
                pool.wait_ge(h2_out[b], 16 * TT // 2)

            last_token, last_row = pool.to_reg(S * 4 - 1), pool.to_reg(S * TOPK * 4 - 1)

            def gather(job):
                for c in range(NCH):
                    pool.indirect_dma_start(xg[:, c, :], None, h2_rows,
                                            bass.IndirectOffsetOnAxis(ap=idx_g[:, c:c + 1], axis=0),
                                            bounds_check=last_token, oob_is_err=False).then_inc(gathered[c], 16)

            pool.wait_ge(xg_zero, 1)
            pool.wait_ge(idx_done, 1)
            gather(0)
            pool.wait_ge(jobs_done, 2)
            njobs = pool.value_load(njobs_i[0:1, 0:1], min_val=E, max_val=JOBS_MAX - 1)
            with pool.Fori(0, njobs) as job:
                pool.wait_ge(idx_done, job + 2)
                pool.wait_ge(x_tr, job * 2 + 2)
                pool.sem_inc(waited_pool, 1)
                gather(job + 1)
                for c in range(NCH):
                    pool.wait_ge(y_done, job * NCH + (c + 2))
                    pool.sem_inc(waited_pool, 1)
                    pool.indirect_dma_start(y_rows, bass.IndirectOffsetOnAxis(ap=idx_s[:, 0, c:c + 1], axis=0),
                                            yb[:, c, :], None, bounds_check=last_row, oob_is_err=False)\
                        .then_inc(scattered[c], 16)
            for c in range(NCH):
                pool.wait_ge(gathered[c], njobs * 16 + 16)

        @block.vector
        def _(dve):
            steps = [0]

            def link(ins):
                ins.then_inc(step, 1)
                steps[0] += 1
                dve.wait_ge(step, steps[0])

            dve.sem_inc(gu_read, 1)
            dve.sem_inc(y_done, 1)
            dve.memset(eps, EPS).then_inc(eps_set, 1)
            dve.memset(relb[BUCKETS:BUCKETS + 1, :], 1.0).then_inc(relb_one, 1)

            def norm(t, phase):
                if t >= 2 or phase:
                    dve.wait_ge(tr_done, 2 * (phase * TT + t - 1))
                if phase and t >= 2:
                    dve.wait_ge(h2_out[t % 2], 16 * (t // 2))
                dve.scalar_tensor_tensor(hbuf[:, t % 2, :], xs[:, t, :], rstd[:, t:t + 1], gain[:, :],
                                         ALU.mult, ALU.mult).then_inc(h_done, 1)

            def copy_h(t, phase):
                dve.wait_ge(tr_done, 2 * (phase * TT + t + 1))
                dve.tensor_copy(hT[:, 4:8, t * P:(t + 1) * P], bank[5][:, :].rearrange("p (k s) -> p k s", k=4))\
                    .then_inc(tr_dve, 1)

            dve.wait_ge(r_mm, 1)
            for a in range(2):
                dve.tensor_copy(r_sb[:, a * RLEN // 2:(a + 1) * RLEN // 2], bank[a][0:HEADS, 0:RLEN // 2])\
                    .then_inc(r_copied, 1)
            dve.wait_ge(sqrt_done, TT)
            link(dve.reciprocal(rstd, rstd))
            dve.wait_ge(gain_in, 16)
            for t in range(TT + 1):
                if t < TT:
                    norm(t, 0)
                if t >= 1:
                    copy_h(t - 1, 0)

            def invert(n):
                dve.wait_ge(exp_done, 2 * (n + 1))
                if n:
                    dve.wait_ge(norm_done, 2 * n)
                dve.reciprocal(row_inv, row_sum).then_inc(inv_done, 1)

            for it in range(PAIRS + 1):
                for i in range(TT):
                    n = TT * it + i
                    if 0 < n <= TT * PAIRS:
                        invert(n - 1)
                    if it >= 1:
                        dve.wait_ge(pt_done, TT * (it - 1) + i + 1)
                        a = tri(i) * P
                        dve.tensor_copy(probT[:, 0, a:a + (i + 1) * P], bank[4][:, 0:(i + 1) * P])\
                            .then_inc(pt_dve, 1)
                    if it < PAIRS:
                        dve.wait_ge(score_done, n + 1)
                        if i == 0:
                            dve.wait_ge(bt_in[it % 2], 16 * (it // 2 + 1))
                        a = tri(i) * P
                        for h in range(2):
                            ins = dve.tensor_tensor_reduce(prob[:, h, a:a + (i + 1) * P], bank[2 + h][:, 0:(i + 1) * P],
                                                           btab[:, it % 2, h, 0:(i + 1) * P][:, ::-1], 1.0, -3e38,
                                                           ALU.add, ALU.max, row_max[:, h:h + 1])
                        ins.then_inc(score_read, 1)
                        dve.wait_ge(score_read, n + 1)
                        dve.tensor_scalar(neg_max, row_max, -1.0, None, ALU.mult).then_inc(negmax_done, 1)

            def residual(t):
                dve.wait_ge(op_done, t + 1)
                for n in range(2):
                    part = xs[:, t, n * 512:(n + 1) * 512]
                    ins = dve.tensor_tensor(part, bank[2 * (t % 2) + n][:, :], part, ALU.add)
                    ins.then_inc(x2_half if n == 0 else x2_done, 1)
                dve.wait_ge(sqrt_done, TT + t + 1)
                link(dve.reciprocal(rstd[:, t:t + 1], rstd[:, t:t + 1]))
                if t == 0:
                    dve.wait_ge(gain_in, 32)
                norm(t, 1)

            def choose(t):
                copy_h(t, 1)
                dve.wait_ge(lg_done, t + 1)
                dve.tensor_copy(logits[:, t, :], bank[6][:, t * E:(t + 1) * E]).then_inc(lg_copied, 1)
                dve.wait_ge(lg_copied, t + 1)
                link(dve.max(top[:, t, :], logits[:, t, :]))
                link(dve.max_index(topi[:, t, :], top[:, t, :], logits[:, t, :]))

            residual(0)
            residual(1)
            choose(0)
            residual(2)
            choose(1)
            residual(3)
            choose(2)
            choose(3)
            link(dve.tensor_copy(topf, topi))
            shape = [P, TT, TOPK, E]
            iota = cst[:, C_IOTA:C_IOTA + E]
            link(dve.tensor_tensor(chose, iota.unsqueeze(1).unsqueeze(1).broadcast_to(shape),
                                   topf[:, :, 0:TOPK].unsqueeze(3).broadcast_to(shape), ALU.is_equal))
            dve.tensor_reduce(mask, chose.rearrange("p t k e -> p t e k"), AX.X, ALU.add).then_inc(mask_done, 1)
            dve.wait_ge(mask_done, 1)
            tok = cst[:, C_TOK:C_TOK + TT * TOPK].rearrange("p (t k) -> p t k", t=TT)
            link(dve.tensor_tensor(chose, chose, tok.unsqueeze(3).broadcast_to(shape), ALU.mult))
            link(dve.tensor_reduce(pos4, chose.rearrange("p t k e -> p t e k"), AX.X, ALU.add))
            for c in range(NCH):
                link(dve.tensor_scalar(slot.rearrange("p (c j s) -> p c j s", c=NCH, j=4)[:, c],
                                       iota.unsqueeze(1).broadcast_to([P, 4, CH]), float(c * CH), None, ALU.add))
            link(dve.tensor_copy(pcol[:, :, 0], cst[:, C_TOK4:C_TOK4 + TT]))
            dve.wait_ge(cst_in, 16)
            link(dve.tensor_scalar(pcol[:, :, 2], cst[:, C_TOK4:C_TOK4 + TT], 0.0, 1.0, ALU.mult, ALU.add))
            dve.wait_ge(tr_done, 4 * TT)
            dve.wait_ge(lg_done, TT)
            dve.memset(xg, 0.0).then_inc(xg_zero, 1)
            dve.wait_ge(rank_mm, 1)
            link(dve.scalar_tensor_tensor(rank, mask, float(-FAR), bank[0][:, 0:TT * E].rearrange("p (t e) -> p t e", t=TT),
                                          ALU.mult, ALU.add))
            dve.wait_ge(cnt_mm, 1)
            link(dve.tensor_copy(cnt, bank[1][:, 0:E]))
            link(dve.tensor_scalar(nblk, cnt, float(P), 1.0, ALU.is_gt, ALU.add))
            for b in range(2, TT):
                link(dve.scalar_tensor_tensor(nblk, cnt, float(b * P), nblk, ALU.is_gt, ALU.add))
            link(dve.tensor_tensor_scan(blk_end, ones[:, 0:E], nblk, 0.0, ALU.mult, ALU.add))
            part = cst[:, C_PART:C_PART + 1]
            link(dve.tensor_scalar(before, blk_end, part, 0.0, ALU.is_le, ALU.add, accum_out=jcol[:, 0:1]))
            link(dve.tensor_tensor_reduce(tmp32, before, nblk, 1.0, 0.0, ALU.mult, ALU.add, jcol[:, 1:2]))
            link(dve.tensor_scalar(jcol[:, 0:1], jcol[:, 0:1], float(E - 1), None, ALU.min))
            link(dve.tensor_scalar(tmp32, iota, jcol[:, 0:1], None, ALU.is_equal))
            link(dve.tensor_tensor_reduce(tmp32, tmp32, cnt, 1.0, 0.0, ALU.mult, ALU.add, jcol[:, 2:3]))
            link(dve.tensor_scalar(jcol[:, 3:4], jcol[:, 1:2], part, float(-P), ALU.subtract, ALU.mult))
            link(dve.tensor_tensor(jcol[:, 4:5], jcol[:, 2:3], jcol[:, 3:4], ALU.subtract))
            link(dve.tensor_scalar(jcol[:, 5:6], jcol[:, 4:5], float(CH), 1.0, ALU.is_gt, ALU.add))
            for c in range(2, NCH):
                link(dve.scalar_tensor_tensor(jcol[:, 5:6], jcol[:, 4:5], float(c * CH), jcol[:, 5:6],
                                              ALU.is_gt, ALU.add))
            for n, col in enumerate((0, 3, 5)):
                ins = dve.tensor_scalar(jdiag[:, n * JOBS_MAX:(n + 1) * JOBS_MAX], ident[:, 0:JOBS_MAX],
                                        jcol[:, col:col + 1], None, ALU.mult)
            ins.then_inc(jdiag_done, 1)
            dve.wait_ge(jobs_mm, 1)
            table = bank[1][:, 0:3 * JOBS_MAX].rearrange("p (r n) -> p r n", r=3)
            link(dve.tensor_copy(jobs_f[:, :, :], table))
            dve.tensor_copy(njobs_i[:, :], blk_end[:, E - 1:E]).then_inc(jobs_done, 1)
            dve.tensor_copy(jobs_i[:, :, :], jobs_f[:, :, :]).then_inc(jobs_done, 1)
            gv = gates.rearrange("p (t k) -> p t k", t=TT)
            dve.tensor_tensor(gv, top[:, :, 0:TOPK], top[:, :, 0:1].broadcast_to([P, TT, TOPK]), ALU.subtract)\
                .then_inc(gate_in, 1)

            def job_columns(e, n, wait):
                wait(dve.tensor_scalar(job_r, rank[:, :, bass.ds(e, 1)].rearrange("p t e -> p (t e)"),
                                       jobs_f[:, 1, bass.ds(n, 1)], float(FAR), ALU.subtract, ALU.add))
                dve.tensor_copy(pcol[:, :, 1], pos4[:, :, bass.ds(e, 1)].rearrange("p t e -> p (t e)"))
                for t in range(TT):
                    ins = dve.tensor_scalar(hot[:, t, :], slot, job_r[:, t:t + 1], None, ALU.is_equal)
                ins.then_inc(hot_done, 1)

            def job_picker(e):
                dve.tensor_copy(pick.rearrange("p (j s) -> p j s", j=4),
                                ident[:, bass.ds(e * 4, 4)].unsqueeze(2).broadcast_to([P, 4, CH]))\
                    .then_inc(pick_done, 1)

            def job_rows(n, wait):
                dve.wait_ge(idx_mm, n + 1)
                wait(dve.tensor_copy(job_p.rearrange("p (c n) -> p c n", n=1).broadcast_to([P, NCH, 1]), bank[7][:, 0:4 * NCH].rearrange("p (c n) -> p c n", c=NCH)[:, :, 2:3]))
                wait(dve.scalar_tensor_tensor(idx_t, job_p.unsqueeze(2).broadcast_to([P, NCH, 2]), float(-SKIP),
                                              bank[7][:, 0:4 * NCH].rearrange("p (c n) -> p c n", c=NCH)[:, :, 0:2],
                                              ALU.mult, ALU.add))
                dve.tensor_scalar(idx_g, idx_t[:, :, 0], cst[:, C_SKIPJ:C_SKIPJ + 1], None, ALU.add)\
                    .then_inc(idx_done, 1)

            job_columns(0, 0, link)
            job_rows(0, link)
            job_picker(0)
            link(dve.tensor_copy(keep_s, idx_t[:, :, 1]))
            njobs = dve.value_load(njobs_i[0:1, 0:1], min_val=E, max_val=JOBS_MAX - 1)
            base = steps[0]
            with dve.Fori(0, njobs) as job:
                inner = [0]

                def link_job(ins):
                    ins.then_inc(step, 1)
                    inner[0] += 1
                    dve.wait_ge(step, job * STEPS + (base + inner[0]))

                e = dve.value_load(jobs_i[0:1, 0, bass.ds(job + 1, 1)], min_val=0, max_val=E - 1)
                job_columns(e, job + 1, link_job)
                job_rows(job + 1, link_job)
                dve.wait_ge(bias_copied, job * 2 + 2)
                for c in range(NCH):
                    b = c % 2
                    gate, up = gu[:, b, 0:Q], gu[:, b, Q:2 * Q]
                    dve.wait_ge(gu_done, job * NCH + (c + 1))
                    dve.tensor_tensor(gu[:, b, :], bank[c][:, :], bt[:, 0:2 * Q], ALU.add).then_inc(gu_read, 1)
                    dve.wait_ge(gu_read, job * NCH + (c + 2))
                    dve.tensor_scalar(gate, gate, LIMIT, None, ALU.min).then_inc(gate_clamped, 1)
                    link_job(dve.tensor_scalar(up, up, LIMIT, -LIMIT, ALU.min, ALU.max))
                    dve.wait_ge(gate_clamped, job * NCH + (c + 1))
                    link_job(dve.scalar_tensor_tensor(up, up, 1.0, gate, ALU.add, ALU.mult))
                    dve.wait_ge(t_done, job * NCH + max(c, 1))
                    dve.wait_ge(sig_done, job * NCH + (c + 1))
                    dve.tensor_tensor(act_q[:, b, :], up, sg[:, b, :], ALU.mult).then_inc(act_done, 1)
                job_picker(e)
                for c in range(NCH):
                    dve.wait_ge(scattered[c], job * 16 + 16)
                link_job(dve.tensor_scalar(idx_s[:, 0, :], keep_s, cst[:, C_SKIPJ:C_SKIPJ + 1], None, ALU.add))
                link_job(dve.tensor_copy(keep_s, idx_t[:, :, 1]))
                for c in range(NCH):
                    dve.wait_ge(dn_done, job * NCH + (c + 1))
                    dve.tensor_tensor(yb[:, c, :], bank[4 + c % 2][:, 0:Q], bt[:, 2 * Q:3 * Q], ALU.add)\
                        .then_inc(y_done, 1)
                assert inner[0] == STEPS

            dve.wait_ge(gate_exp, 1)
            total = [0]

            def link_end(ins):
                ins.then_inc(step, 1)
                total[0] += 1
                dve.wait_ge(step, njobs * STEPS + (base + total[0]))

            link_end(dve.tensor_reduce(gsum, gv, AX.X, ALU.add))
            link_end(dve.reciprocal(ginv, gsum))
            link_end(dve.tensor_tensor(gv, gv, ginv.unsqueeze(2).broadcast_to([P, TT, TOPK]), ALU.mult))
            dve.wait_ge(gain_in, 48)
            for t in range(TT):
                dve.wait_ge(y_in[t], 16)
                rows = ring[:, 3 * t:3 * t + 2, :].rearrange("p a (k d) -> p (a k) d", k=2)
                for k in range(TOPK):
                    ins = dve.scalar_tensor_tensor(xs[:, t, :], rows[:, k, :], gv[:, t, k:k + 1], xs[:, t, :],
                                                   ALU.mult, ALU.add)
                    if k < TOPK - 1:
                        link_end(ins)
                ins.then_inc(sum_done, 1)
                dve.wait_ge(sqrt_done, 2 * TT + t + 1)
                link_end(dve.reciprocal(rstd[:, t:t + 1], rstd[:, t:t + 1]))
                dve.scalar_tensor_tensor(ring[:, 3 * t + 2, 0:D], xs[:, t, :], rstd[:, t:t + 1], gain[:, :],
                                         ALU.mult, ALU.mult).then_inc(fin_done, 1)


STEPS = 5 + 2 * NCH


def kernel(x, norm1_g, w_in, pool_w, pool_scale, rel_bias, w_out, norm2_g, router_w, router_b,
           w_gate_up, b_gate_up, w_down, b_down, final_g):
    import concourse.bacc as bacc
    from concourse.bass_utils import run_bass_kernel_spmd

    def a(t):
        return np.ascontiguousarray(np.asarray(t))

    wi = a(w_in)[0]
    q0, k0, v0 = POOL_W, POOL_W + ATT_W, POOL_W + 2 * ATT_W
    pair = [np.concatenate([wi[:, q0 + P * i:q0 + P * (i + 1)], wi[:, k0 + P * i:k0 + P * (i + 1)]], 1)
            for i in range(PAIRS)]
    units = [wi[:, 0:POOL_W], pair[0]] + [wi[:, v0 + 256 * i:v0 + 256 * (i + 1)] for i in range(3)] + pair[1:]
    units = np.stack([u.reshape(KT, P, 256).transpose(1, 0, 2).reshape(P, UNIT) for u in units])
    biases = np.concatenate([a(b_gate_up)[0].reshape(E, 2, 4, Q).transpose(0, 2, 1, 3).reshape(E * 4, 2 * Q),
                             a(b_down)[0].reshape(E * 4, Q)], 1)
    cst, sel = constants()
    ins = {
        "x": a(x)[0], "w_in": units, "w_out": a(w_out)[0],
        "norm1": a(norm1_g)[0], "norm2": a(norm2_g)[0], "final_g": a(final_g),
        "rel_bias": a(rel_bias),
        "pool_w": a(pool_w)[0].reshape(2, 2, PG, PG).transpose(1, 2, 0, 3).reshape(P, 2, PG),
        "pool_scale": a(pool_scale)[0].reshape(2, P).T,
        "router_w": a(router_w)[0].reshape(KT, P, E).transpose(1, 0, 2), "router_b": a(router_b),
        "w_gate_up": a(w_gate_up)[0], "w_down": a(w_down)[0], "biases": biases,
        "consts": cst, "selector": sel,
    }
    nc = bacc.Bacc("TRN2", target_bir_lowering=False, num_devices=1)
    arrays, args = {}, []
    for name, t in ins.items():
        t = np.ascontiguousarray(t)
        arrays[f"in_{name}"] = t
        args.append(nc.dram_tensor(f"in_{name}", t.shape, mybir.dt.from_np(t.dtype), kind="ExternalInput").ap())
    out = nc.dram_tensor("out_0", (S, D), F32, kind="ExternalOutput").ap()
    program(nc, *args, out)
    r = run_bass_kernel_spmd(nc, [arrays], core_ids=[0])
    return r.results[0]["out_0"].reshape(1, S, D)
```

```python
import math
from contextlib import ExitStack

import concourse.bass as bass
import numpy as np
from concourse import mybir

F32 = mybir.dt.float32
F16 = mybir.dt.float16
I32 = mybir.dt.int32
U32 = mybir.dt.uint32
ALU = mybir.AluOpType
ACT = mybir.ActivationFunctionType
AX = mybir.AxisListType

P = 128
D = 1024
S = 512
TT = S // P
KT = D // P
POOL_W = 256
WINDOWS = (2, 4, 8, 16)
PG = POOL_W // 4
HEADS = 12
DH = 64
PAIRS = HEADS // 2
ATT_W = HEADS * DH
BUCKETS = 32
MAX_DIST = 2048
BRANCHES = ((128, 1), (512, 4), (2048, 16))
E = 32
TOPK = 4
FF = 1024
EPS = 1e-5
LIMIT = 7.0
ALPHA = 1.702
MASKED = -1e30

CH = 32
NCH = P // CH
Q = D // 4
UNIT = 2048
RING = 18
MIX_RING = 12
HALF = 6
MIXR = KT * S + 64
WORK = 12288
IN_UNITS = 10
OUT_UNITS = 4
PRE = IN_UNITS + OUT_UNITS
JOB_UNITS = 12
FREED = JOB_UNITS - 2
JOBS_MAX = 49
FAR = 4096
SKIP = 16384
RLEN = 640

C_ID, C_TRI, C_ONE = 0, 128, 256
C_IOTA = 384
C_TOK = 416
C_CNT = 432
C_INVW = 464
C_SKIPJ = 466
C_PART = 467
C_TOK4 = 468
C_FIRST = 472
C_PHASE = 473
C_END = 474


def bucket_of(dist):
    exact = BUCKETS // 2
    nf = np.maximum(dist, 1).astype(np.float32)
    large = exact + (np.log(nf / np.float32(exact)) / np.float32(math.log(MAX_DIST / exact))
                     * np.float32(BUCKETS - exact)).astype(np.int32)
    return np.where(dist < exact, dist, np.minimum(large, BUCKETS - 1))


def constants():
    c = np.zeros((P, C_END), np.float32)
    p = np.arange(P)
    c[:, C_ID:C_ID + P] = np.eye(P)
    c[:, C_TRI:C_TRI + P] = p[:, None] < p[None, :]
    c[:, C_ONE:C_ONE + P] = 1.0
    c[:, C_IOTA:C_IOTA + E] = np.arange(E)
    tok = np.arange(TT)[None, :] * P + p[:, None]
    c[:, C_TOK:C_TOK + TT * TOPK] = (16 * tok[:, :, None] + 4 * np.arange(TOPK)).reshape(P, -1)
    for m in range(2):
        w = np.where(p < PG, WINDOWS[2 * m], WINDOWS[2 * m + 1]).astype(np.float32)
        cnt = np.minimum(np.arange(16)[None, :] + 1, w[:, None]).astype(np.float32)
        c[:, C_CNT + 16 * m:C_CNT + 16 * (m + 1)] = w[:, None] / cnt
        c[:, C_INVW + m] = 1.0 / w
    c[:, C_SKIPJ] = SKIP + p // CH
    c[:, C_PART] = p
    c[:, C_FIRST] = np.where(p < E, p, 0)
    c[:, C_PHASE] = NCH * (p * JOB_UNITS // HALF % (RING // HALF))
    c[:, C_TOK4:C_TOK4 + TT] = 4 * tok
    dist = np.arange(RLEN) - (P - 1)
    count = sum(((dist % dil == 0) & (dist <= window)).astype(np.float64) for window, dil in BRANCHES)
    seen = (dist >= 0) & (count > 0)
    sel = np.zeros((BUCKETS + 1, RLEN), np.float32)
    sel[bucket_of(np.maximum(dist, 0))[seen], np.arange(RLEN)[seen]] = 1.0
    sel[BUCKETS] = np.where(seen, np.log(np.maximum(count, 1)), MASKED)
    return c, sel


def tri(i):
    return i * (i + 1) // 2


def program(nc, x, w_in, w_out, norm1, norm2, final_g, rel_bias, pool_w, pool_scale, router_w,
            router_b, w_gate_up, w_down, biases, consts, selector, turn_table, out):
    xv = x.rearrange("(t p) d -> t p d", p=P)
    outv = out.rearrange("(t p) d -> t p d", p=P)
    bias_by_dist = nc.dram_tensor("bias_by_dist", [HEADS, RLEN], F32).ap()
    h2_rows = nc.dram_tensor("h2_rows", [S * 4, Q], F32).ap()
    y_rows = nc.dram_tensor("y_rows", [S * TOPK * 4, Q], F32).ap()

    with ExitStack() as ctx:
        def sb(name, shape, dt=F32):
            return ctx.enter_context(nc.sbuf_tensor(name, shape, dt))

        def sem(name):
            return ctx.enter_context(nc.semaphore(name))

        bank = [ctx.enter_context(nc.psum_tensor(f"bank{i}", [P, 512], F32)) for i in range(8)]

        arena = sb("arena", [P, MIX_RING * UNIT + MIXR + WORK])
        ring = arena[:, 0:RING * UNIT].rearrange("p (s n) -> p s n", s=RING)
        xs = sb("xs", [P, TT, D])
        hT = sb("hT", [P, KT, S])
        mixr = arena[:, MIX_RING * UNIT:MIX_RING * UNIT + MIXR]
        mixT = mixr[:, 0:KT * S].rearrange("p (k s) -> p k s", k=KT)
        gain = sb("gain", [P, D])
        cst = sb("cst", [P, C_END])
        rw = sb("rw", [P, KT, E])
        bias_all = sb("bias_all", [P, 3 * Q])
        rb = sb("rb", [1, E])
        relb = sb("relb", [BUCKETS + 1, HEADS])
        pw = sb("pw", [P, 2, PG])
        pscale = sb("pscale", [P, 2])
        work = arena[:, MIX_RING * UNIT + MIXR:]

        ident = cst[:, C_ID:C_ID + P]
        tri_c = cst[:, C_TRI:C_TRI + P]
        ones = cst[:, C_ONE:C_ONE + P]

        st = sb("st", [P, 96])
        ssq, rstd = st[:, 0:4], st[:, 4:8]
        neg_max, row_sum, row_inv = st[:, 8:10], st[:, 10:12], st[:, 12:14]
        row_max = st[:, 14:16]
        eps = st[:, 16:17]
        gates, gsum, ginv = st[:, 20:36], st[:, 36:40], st[:, 40:44]
        job_r, job_p, keep_s = st[:, 44:48], st[:, 48:52], st[:, 52:56]

        qk = work[:, 0:2048].rearrange("p (b w s) -> p b w s", b=2, w=2)
        v = work[:, 2048:5120].rearrange("p (t c) -> p t c", t=TT)
        prob = work[:, 5120:7680].rearrange("p (h n) -> p h n", h=2)
        probT = work[:, 7680:10240].rearrange("p (h n) -> p h n", h=2)
        btab = work[:, 10240:12288].rearrange("p (b h n) -> p b h n", b=2, h=2)
        hbuf = work[:, 5120:7168].rearrange("p (b d) -> p b d", b=2)
        sq_junk = work[:, 7680:8704]
        r_sb = work[0:HEADS, 8704:8704 + RLEN]
        sel_sb = work[0:BUCKETS + 1, 9344:9344 + RLEN]
        pa = mixr[:, 1024:1024 + 1040].rearrange("p (m s) -> p m s", m=2)
        pb = mixr[:, 2064:2064 + 1040].rearrange("p (m s) -> p m s", m=2)
        pc = mixr[:, 3104:3104 + 1040].rearrange("p (m s) -> p m s", m=2)

        o = 8704
        logits = work[:, o:o + 128].rearrange("p (t e) -> p t e", t=TT)
        top = work[:, o + 128:o + 160].rearrange("p (t k) -> p t k", t=TT)
        topi = work[:, o + 160:o + 192].bitcast(U32).rearrange("p (t k) -> p t k", t=TT)
        topf = work[:, o + 192:o + 224].rearrange("p (t k) -> p t k", t=TT)
        chose = work[:, o + 224:o + 736].rearrange("p (t k e) -> p t k e", t=TT, k=TOPK)
        mask = work[:, o + 736:o + 800].bitcast(F16).rearrange("p (t e) -> p t e", t=TT)
        tri16 = work[:, 11568:11632].bitcast(F16)
        ones16 = work[:, 11632:11696].bitcast(F16)
        rank = work[:, o + 864:o + 992].rearrange("p (t e) -> p t e", t=TT)
        pos4 = work[:, o + 992:o + 1120].rearrange("p (t e) -> p t e", t=TT)
        cnt = work[:, o + 1120:o + 1152]
        nblk = work[:, o + 1152:o + 1184]
        tmp32 = work[:, o + 1184:o + 1216]
        blk_end = work[:, o + 1216:o + 1248]
        before = work[:, o + 1248:o + 1280]
        jcol = work[:, o + 1280:o + 1296]
        jdiag = work[:, o + 1296:o + 1296 + 4 * JOBS_MAX]
        jobs_f = sb("jobs_f", [P, 4, JOBS_MAX])
        jobs_i = sb("jobs_i", [P, 4, JOBS_MAX], I32)
        njobs_i = sb("njobs_i", [P, 1], I32)
        turns = sb("turns_sb", [1, 2 * JOBS_MAX], I32)
        ahead = sb("ahead", [16, 2, NCH, 4])

        gu = work[:, 8128:9152].rearrange("p (b n) -> p b n", b=2)
        sg = work[:, 11568:12080].rearrange("p (b n) -> p b n", b=2)
        pick = work[:, 12080:12208]
        bt = gain[:, 0:3 * Q]
        act_q = [gain[:, 3 * Q:D], work[:, 9152:9152 + Q]]
        yb = hT[:, 6:8, :].rearrange("p a (c n) -> p (a c) n", c=2)
        final_gain = ring[:, MIX_RING, 0:D]
        hot = work[:, 10240:11264].bitcast(F16).rearrange("p (t n) -> p t n", t=TT)
        slot = work[:, 11264:11520].bitcast(F16)
        pcol = work[:, 11520:11528].bitcast(F16)[:, 0:3 * TT].rearrange("p (t n) -> p t n", t=TT)
        idx_t = work[:, 11536:11544].rearrange("p (c n) -> p c n", c=NCH)
        idx_g = work[:, 11552:11556].bitcast(U32)
        idx_s = work[:, 11560:11564].bitcast(U32)
        xg = hT[:, 0:2, :].rearrange("p a (c n) -> p (a c) n", c=2)
        xT = hT[:, 2:4, :].rearrange("p a (c n) -> p (a c) n", c=2)
        aT = hT[:, 4:6, :].rearrange("p a (c n) -> p (a c) n", c=2)

        cst_in, small_in, gain_in = sem("cst_in"), sem("small_in"), sem("gain_in")
        x_in = [sem(f"x_in{t}") for t in range(TT)]
        mix_full = [sem(f"mix_full{s}") for s in range(MIX_RING)]
        unit_full = [sem(f"unit_full{u}") for u in range(JOB_UNITS)]
        turns_in = sem("turns_in")
        units_used = sem("units_used")
        eps_set, table_in = sem("eps_set"), sem("table_in")
        ssq_done = sem("ssq_done")
        sqrt_done = sem("sqrt_done")
        h_done = sem("h_done")
        tr_done = sem("tr_done")
        tr_act = sem("tr_act")
        tr_dve = sem("tr_dve")
        relb_one = sem("relb_one")
        r_mm, r_copied, r_out = sem("r_mm"), sem("r_copied"), sem("r_out")
        bt_in = [sem(f"bt_in{b}") for b in range(2)]
        proj_done = sem("proj_done")
        proj_act = sem("proj_act")
        u_pad = sem("u_pad")
        pooled = sem("pooled")
        poolmm = sem("poolmm")
        pool_out = sem("pool_out")
        score_done = sem("score_done")
        score_read = sem("score_read")
        negmax_done = sem("negmax_done")
        exp_done = sem("exp_done")
        inv_done = sem("inv_done")
        norm_done = sem("norm_done")
        pt_done = sem("pt_done")
        pt_dve, pt_act = sem("pt_dve"), sem("pt_act")
        pv_done = sem("pv_done")
        att_out = sem("att_out")
        op_done = sem("op_done")
        out_used = sem("out_used")
        x2_done = sem("x2_done")
        h2_out = [sem(f"h2_out{b}") for b in range(2)]
        lg_done, lg_copied = sem("lg_done"), sem("lg_copied")
        step = sem("step")
        mask_done = sem("mask_done")
        rank_mm, cnt_mm = sem("rank_mm"), sem("cnt_mm")
        jdiag_done, jobs_mm, jobs_done = sem("jdiag_done"), sem("jobs_mm"), sem("jobs_done")
        gate_in, gate_exp = sem("gate_in"), sem("gate_exp")
        xg_zero = sem("xg_zero")
        hot_done = sem("hot_done")
        pick_done = sem("pick_done")
        idx_mm = sem("idx_mm")
        idx_done = sem("idx_done")
        gathered = [sem(f"gathered{c}") for c in range(NCH)]
        x_tr, x_copied = sem("x_tr"), sem("x_copied")
        bias_mm, bias_copied = sem("bias_mm"), sem("bias_copied")
        gu_done = sem("gu_done")
        gu_read = sem("gu_read")
        gate_clamped, sig_done, act_done = sem("gate_clamped"), sem("sig_done"), sem("act_done")
        t_done, t_copied = sem("t_done"), sem("t_copied")
        dn_done, y_done = sem("dn_done"), sem("y_done")
        scattered = [sem(f"scattered{c}") for c in range(NCH)]
        y_in = [[sem(f"y_in{t}_{a}") for a in range(2)] for t in range(TT)]
        sum_done, fin_done, out_done = sem("sum_done"), sem("fin_done"), sem("out_done")
        pstep = sem("pstep")
        waited_sp, waited_pool = sem("waited_sp"), sem("waited_pool")

        def mix_slot(n):
            return (n + MIX_RING - IN_UNITS + KT) % MIX_RING

        def half_slot(eng, job, half):
            return eng.value_load(turns[0:1, bass.ds(job * 2 + half, 1)], min_val=0, max_val=RING - HALF)

        block = ctx.enter_context(nc.Block())

        @block.sync
        def _(sp):
            for t in range(TT):
                sp.dma_start(xs[:, t, :], xv[t]).then_inc(x_in[t], 16)
                if t == 0:
                    sp.dma_start(cst[:, :], consts).then_inc(cst_in, 16)
            for n in range(PRE):
                if n >= MIX_RING:
                    sp.wait_ge(proj_done, 2 * (n - MIX_RING + 1))
                s = mix_slot(n)
                if n < IN_UNITS:
                    src = w_in[n]
                else:
                    a = (n - IN_UNITS) * 2 * P
                    src = w_out[a:a + 2 * P, :].rearrange("(k p) n -> p k n", p=P)
                dst = ring[:, s, :] if n < IN_UNITS else ring[:, s, :].rearrange("p (k n) -> p k n", k=2)
                sp.dma_start(dst, src).then_inc(mix_full[s], 16)
                if n == 1:
                    for dst, src in ((relb[0:BUCKETS, :], rel_bias), (sel_sb, selector), (rw[:, :, :], router_w),
                                     (bias_all[:, :], biases), (rb[:, :], router_b), (pw[:, :, :], pool_w),
                                     (pscale[:, :], pool_scale)):
                        sp.dma_start(dst, src).then_inc(small_in, 16)
            sp.dma_start(turns[:, :], turn_table).then_inc(turns_in, 16)

            def wait_read(job, u):
                if u == KT - 1:
                    sp.wait_ge(gu_done, job * NCH + NCH)
                elif u == JOB_UNITS - 1:
                    sp.wait_ge(dn_done, job * NCH + NCH)
                else:
                    sp.wait_ge(units_used, job * FREED + (u + 1 - (u >= KT)))

            def load_unit(e, u, slot):
                if u < KT:
                    src = w_gate_up[bass.ds(e, 1), u * P:(u + 1) * P, :].rearrange("e p n -> p (e n)")
                    dst = ring[:, bass.ds(slot, 1), :].rearrange("p s n -> p (s n)")
                else:
                    a = (u - KT) * 2 * P
                    src = w_down[bass.ds(e, 1), a:a + 2 * P, :].rearrange("e (k p) n -> p (e k) n", p=P)
                    dst = ring[:, bass.ds(slot, 1), :].rearrange("p s (k n) -> p (s k) n", k=2)
                sp.dma_start(dst, src).then_inc(unit_full[u], 16)

            def load_job(e, job, slots):
                for u in range(JOB_UNITS):
                    if u >= RING - JOB_UNITS:
                        wait_read(job - 1, u - (RING - JOB_UNITS))
                    else:
                        wait_read(job - 2, u + 2 * JOB_UNITS - RING)
                    sp.sem_inc(waited_sp, 1)
                    sp.wait_ge(unit_full[u], job * 16)
                    sp.sem_inc(waited_sp, 1)
                    load_unit(e, u, slots[u // HALF] + u % HALF)

            def first_unit(n):
                if n >= JOB_UNITS:
                    sp.wait_ge(unit_full[n - JOB_UNITS], 16)
                load_unit(n // JOB_UNITS, n % JOB_UNITS, n)

            for n in range(KT):
                sp.wait_ge(proj_done, 2 * (IN_UNITS - KT + n + 1))
                first_unit(n)
            sp.wait_ge(pv_done, PAIRS)
            first_unit(14)
            first_unit(15)
            for n in (8, 9, 10):
                sp.wait_ge(out_used, n - KT + 1)
                first_unit(n)
            sp.wait_ge(op_done, TT)
            for b in range(2):
                sp.wait_ge(h2_out[b], 16 * TT // 2)
            for n in (11, 12, 13):
                first_unit(n)
            for c in range(NCH):
                sp.wait_ge(gathered[c], 16)
            first_unit(16)
            first_unit(17)
            for u in range(HALF, JOB_UNITS):
                wait_read(0, u - HALF)
                sp.wait_ge(unit_full[u], 16)
                load_unit(1, u, u - HALF)
            sp.wait_ge(jobs_done, 2)
            sp.wait_ge(turns_in, 16)
            njobs = sp.value_load(njobs_i[0:1, 0:1], min_val=E, max_val=JOBS_MAX - 2)
            all_out, all_down = sp.snap(njobs * 16 + 16), sp.snap(njobs * NCH)
            with sp.Fori(2, njobs) as job:
                e = sp.value_load(jobs_i[0:1, 0, bass.ds(job, 1)], min_val=0, max_val=E - 1)
                load_job(e, job, [half_slot(sp, job, 0), half_slot(sp, job, 1)])
            for c in range(NCH):
                sp.wait_ge(scattered[c], all_out)
                sp.sem_inc(waited_sp, 1)
            sp.wait_ge(dn_done, all_down)
            yv = y_rows.rearrange("(t p r) q -> t p (r q)", t=TT, p=P)
            for t in range(TT):
                for a in range(2):
                    sp.dma_start(ring[:, 3 * t + a, :], yv[t][:, a * UNIT:(a + 1) * UNIT]).then_inc(y_in[t][a], 16)
            for t in range(TT):
                for a in range(2):
                    c = slice(a * D // 2, (a + 1) * D // 2)
                    sp.wait_ge(fin_done, 2 * t + a + 1)
                    sp.dma_start(outv[t][:, c], ring[:, 3 * t + 2, c]).then_inc(out_done, 16)
            sp.wait_ge(out_done, 16 * TT * 2)

        @block.tensor
        def _(pe):
            pe.sem_inc(t_done, 1)
            pe.wait_ge(cst_in, 16)

            def transposes(src, groups):
                for g in range(2):
                    if groups >= 2:
                        pe.wait_ge(tr_act if g == 0 else tr_dve, groups // 2)
                    for k in range(4):
                        mm = pe.transpose(bank[4 + g][:, k * P:(k + 1) * P],
                                          src[:, (4 * g + k) * P:(4 * g + k + 1) * P], ident)
                    mm.then_inc(tr_done, 1)

            for t in range(TT):
                pe.wait_ge(h_done, t + 1)
                transposes(hbuf[:, t % 2, :], 2 * t)
            pe.wait_ge(tr_act, TT)
            pe.wait_ge(tr_dve, TT)

            groups = [0]

            def projection_bank():
                n = groups[0]
                groups[0] += 1
                if n >= 2:
                    pe.wait_ge(proj_act, n - 1)
                return bank[n % 2]

            def project_unit(unit):
                pe.wait_ge(mix_full[mix_slot(unit)], 16)
                for half in range(2):
                    w = ring[:, mix_slot(unit), :].rearrange("p (k n) -> p k n", k=KT)
                    b = projection_bank()
                    for k in range(KT):
                        mm = pe.matmul(b[:, :], w[:, k, half * P:(half + 1) * P], hT[:, k, :],
                                       start=(k == 0), stop=(k == KT - 1))
                        if k == KT - 1:
                            mm.then_inc(proj_done, 1)
                        if k % 4 == 3:
                            yield

            def project_values(unit):
                pe.wait_ge(mix_full[mix_slot(unit)], 16)
                w = ring[:, mix_slot(unit), :].rearrange("p (k n) -> p k n", k=KT)
                for tp in range(2):
                    b = projection_bank()
                    for half in range(2):
                        t = 2 * tp + half
                        for k in range(KT):
                            mm = pe.matmul(b[:, half * 256:(half + 1) * 256], hT[:, k, t * P:(t + 1) * P], w[:, k, :],
                                           start=(k == 0), stop=(k == KT - 1))
                    mm.then_inc(proj_done, 1)

            def scores(pr, i):
                n = TT * pr + i
                if n >= 1:
                    pe.wait_ge(score_read, n)
                else:
                    pe.wait_ge(r_copied, 2)
                for h in range(2):
                    r = slice(h * DH, (h + 1) * DH)
                    mm = pe.matmul(bank[2 + h][:, 0:(i + 1) * P], qk[r, pr % 2, 0, i * P:(i + 1) * P],
                                   qk[r, pr % 2, 1, 0:(i + 1) * P], start=True, stop=True)
                mm.then_inc(score_done, 1)

            def flip(pr, i):
                n = TT * pr + i
                pe.wait_ge(norm_done, 2 * (n + 1))
                if n >= 1:
                    pe.wait_ge(pt_dve, n)
                    pe.wait_ge(pt_act, n)
                for h in range(2):
                    for kb in range(i + 1):
                        a = (tri(i) + kb) * P
                        mm = pe.transpose(bank[4 + h][:, kb * P:(kb + 1) * P], prob[:, h, a:a + P], ident)
                mm.then_inc(pt_done, 1)

            def values(pr, i):
                n = TT * pr + i
                pe.wait_ge(pt_dve, n + 1)
                pe.wait_ge(pt_act, n + 1)
                if i == 0 and pr >= 1:
                    pe.wait_ge(att_out, pr)
                for kb in range(i + 1):
                    for h in range(2):
                        a = (tri(i) + kb) * P
                        c = (2 * pr + h) * DH
                        mm = pe.matmul(bank[6][h * DH:(h + 1) * DH, i * P:(i + 1) * P], v[:, kb, c:c + DH],
                                       probT[:, h, a:a + P], start=(kb == 0), stop=(kb == i))
                if i == TT - 1:
                    mm.then_inc(pv_done, 1)

            def project_out(t, n, ks):
                b = bank[2 * (t % 2) + n][:, :]
                for k in ks:
                    s = mix_slot(IN_UNITS + k // 2)
                    if t == 0 and n == 0 and k % 2 == 0:
                        pe.wait_ge(mix_full[s], 16 * ((IN_UNITS + k // 2) // MIX_RING + 1))
                    c = (k % 2) * D + n * 512
                    mm = pe.matmul(b, mixT[:, k, t * P:(t + 1) * P], ring[:, s, c:c + 512],
                                   start=(k == 0), stop=(k == KT - 1))
                    if n == 1 and k == KT - 1:
                        mm.then_inc(op_done, 1)
                    elif t == TT - 1 and n == 1 and k % 2 == 1:
                        mm.then_inc(out_used, 1)

            def spare(t):
                if t == 0:
                    pe.wait_ge(proj_act, 2 * IN_UNITS)
                    pe.wait_ge(pool_out, 2)
                    pe.wait_ge(att_out, PAIRS - 2)
                else:
                    pe.wait_ge(score_read, TT * PAIRS)
                for q in range(3):
                    for n in range(2):
                        project_out(t, n, range(2 * q, 2 * q + 2))
                    yield
                if t == 1:
                    pe.wait_ge(att_out, PAIRS - 1)
                    for tile in range(2):
                        for n in range(2):
                            project_out(tile, n, range(KT - 2, KT - 1))
                yield

            for _ in project_unit(0):
                pass
            pe.wait_ge(small_in, 16 * 7)
            pe.wait_ge(relb_one, 1)
            for a in range(2):
                mm = pe.matmul(bank[2 + a][0:HEADS, 0:RLEN // 2], relb[:, :],
                               sel_sb[:, a * RLEN // 2:(a + 1) * RLEN // 2], start=True, stop=True)
            mm.then_inc(r_mm, 1)
            for _ in project_unit(1):
                pass
            for i in range(3):
                project_values(2 + i)
            for it in range(PAIRS + 1):
                ahead = project_unit(5 + it) if it + 1 < PAIRS else spare(it + 1 - PAIRS)
                for i in range(TT):
                    next(ahead)
                    if it >= 1:
                        flip(it - 1, i)
                    if it < PAIRS:
                        if i == 0:
                            pe.wait_ge(proj_act, 2 + 2 + 6 + 2 * it)
                        scores(it, i)
                    if it >= 1:
                        values(it - 1, i)
                for _ in ahead:
                    pass
                if it == 0:
                    pe.wait_ge(pooled, 4)
                    for m in range(2):
                        if m:
                            pe.wait_ge(pool_out, 1)
                        for g in range(2):
                            r = slice(g * PG, (g + 1) * PG)
                            mm = pe.matmul(bank[7][r, :], pw[r, m, :], pa[r, m, 8:8 + S], start=True, stop=True)
                        mm.then_inc(poolmm, 1)

            def flip_h2(t):
                pe.wait_ge(h_done, TT + t + 1)
                transposes(hbuf[:, t % 2, :], 2 * (TT + t))

            def route(t):
                pe.wait_ge(tr_act, TT + t + 1)
                pe.wait_ge(tr_dve, TT + t + 1)
                if t >= 1:
                    pe.wait_ge(lg_copied, t)
                out_ = bank[6][:, t * E:(t + 1) * E]
                for k in range(KT):
                    pe.matmul(out_, hT[:, k, t * P:(t + 1) * P], rw[:, k, :], start=(k == 0), stop=False)
                pe.matmul(out_, ones[0:1, :], rb[:, :], start=False, stop=True).then_inc(lg_done, 1)

            pe.wait_ge(pool_out, 2)
            pe.wait_ge(att_out, PAIRS)
            pe.wait_ge(pt_dve, TT * PAIRS)
            pe.wait_ge(pt_act, TT * PAIRS)
            for n in range(2):
                project_out(0, n, range(KT - 1, KT))
            for n in range(2):
                project_out(1, n, range(KT - 1, KT))
            pe.wait_ge(x2_done, 1)
            project_out(2, 0, range(KT))
            flip_h2(0)
            project_out(2, 1, range(KT))
            route(0)
            flip_h2(1)
            pe.wait_ge(x2_done, 2)
            for k in range(0, KT, 2):
                for n in range(2):
                    project_out(3, n, range(k, k + 2))
                if k == 2:
                    route(1)
                    flip_h2(2)
            route(2)
            flip_h2(3)
            route(3)
            pe.wait_ge(mask_done, TT)
            for t in range(TT):
                for u in range(t + 1):
                    mm = pe.matmul(bank[0][:, t * E:(t + 1) * E], tri16 if u == t else ones16, mask[:, u, :],
                                   start=(u == 0), stop=(u == t))
            mm.then_inc(rank_mm, 1)
            for t in range(TT):
                mm = pe.matmul(bank[1][:, 0:E], ones16, mask[:, t, :], start=(t == 0), stop=(t == TT - 1))
            mm.then_inc(cnt_mm, 1)

            def indices(job):
                pe.wait_ge(hot_done, job + 1)
                for c in range(NCH):
                    for t in range(TT):
                        mm = pe.matmul(bank[7][:, 4 * c:4 * c + 3], hot[:, t, c * P:(c + 1) * P], pcol[:, t, :],
                                       start=(t == 0), stop=(t == TT - 1))
                mm.then_inc(idx_mm, 1)

            def flip_x(job, a):
                for c in (2 * a, 2 * a + 1):
                    pe.wait_ge(gathered[c], job * 16 + 16)
                if a == 1:
                    pe.wait_ge(x_copied, job * 2 + 1)
                for c in range(2):
                    for h in range(2):
                        mm = pe.transpose(bank[7][:, c * Q + h * P:c * Q + (h + 1) * P],
                                          xg[:, 2 * a + c, h * P:(h + 1) * P], ident)
                mm.then_inc(x_tr, 1)

            indices(0)
            pe.wait_ge(jdiag_done, 1)
            pe.matmul(bank[1][:, 0:4 * JOBS_MAX], ones, jdiag, start=True, stop=True).then_inc(jobs_mm, 1)
            pe.wait_ge(idx_done, 1)
            flip_x(0, 0)
            flip_x(0, 1)
            pe.wait_ge(jobs_done, 2)

            def run_job(job, m, first):
                def gate_up(c, k):
                    w = ring[:, (first + k) % RING, :].rearrange("p (g n) -> p g n", g=2)
                    for j in range(4):
                        mm = pe.matmul(bank[c][j * CH:(j + 1) * CH, :].rearrange("p (g n) -> p g n", g=2),
                                       xT[:, c, (k % 2) * P + (k // 2) * CH:(k % 2) * P + (k // 2 + 1) * CH],
                                       w[:, :, j * Q:(j + 1) * Q], start=(k == 0), stop=(k == KT - 1),
                                       tile_position=(0, j * CH))
                    return mm

                for k in range(KT // 2):
                    pe.wait_ge(unit_full[k], job * 16 + 16)
                    for c in range(m):
                        mm = gate_up(c, k)
                    mm.then_inc(units_used, 1)
                    if k == 0:
                        indices(job + 1)
                    if k == 1:
                        pe.wait_ge(idx_done, job + 2)
                        pe.wait_ge(pick_done, job + 1)
                        pe.matmul(bank[7][:, 0:2 * Q], pick, bias_all[:, 0:2 * Q], start=True, stop=True)\
                            .then_inc(bias_mm, 1)
                    if k == 2:
                        pe.wait_ge(bias_copied, job * 2 + 1)
                        pe.matmul(bank[7][:, 0:Q], pick, bias_all[:, 2 * Q:3 * Q], start=True, stop=True)\
                            .then_inc(bias_mm, 1)
                for c in range(m):
                    for k in range(KT // 2, KT):
                        if c == 0:
                            pe.wait_ge(unit_full[k], job * 16 + 16)
                        mm = gate_up(c, k)
                        if c == m - 1 and k < KT - 1:
                            mm.then_inc(units_used, 1)
                    mm.then_inc(gu_done, 1 if c < m - 1 else NCH - m + 1)

                def flip_act(c):
                    pe.wait_ge(act_done, job * NCH + (c + 1))
                    pe.wait_ge(t_copied, job * NCH + (c + 1))
                    for h in range(2):
                        mm = pe.transpose(bank[6][:, h * P:(h + 1) * P], act_q[c % 2][:, h * P:(h + 1) * P], ident)
                    mm.then_inc(t_done, 1 if c < m - 1 else NCH - m + 1)

                flip_act(0)
                pe.wait_ge(y_done, job * NCH + 1)
                for c in range(m):
                    pe.wait_ge(t_copied, job * NCH + (c + 2))
                    if c >= 2:
                        pe.wait_ge(y_done, job * NCH + c)
                    for k in range(KT):
                        u = KT + k // 2
                        if c == 0 and k % 2 == 0:
                            pe.wait_ge(unit_full[u], job * 16 + 16)
                        w = ring[:, (first + u) % RING, (k % 2) * D:(k % 2 + 1) * D]
                        for j in range(4):
                            mm = pe.matmul(bank[4 + c % 2][j * CH:(j + 1) * CH, 0:Q],
                                           aT[:, c, (k % 2) * P + (k // 2) * CH:(k % 2) * P + (k // 2 + 1) * CH],
                                           w[:, j * Q:(j + 1) * Q], start=(k == 0), stop=(k == KT - 1),
                                           tile_position=(0, j * CH))
                        if c == m - 1 and k % 2 == 1 and k < KT - 1:
                            mm.then_inc(units_used, 1)
                        if k == 4 and c + 1 < m:
                            flip_act(c + 1)
                        if k == 6 and c == 1:
                            flip_x(job + 1, 1)
                    mm.then_inc(dn_done, 1 if c < m - 1 else NCH - m + 1)
                    if c == 0:
                        pe.wait_ge(bias_copied, job * 2 + 2)
                        flip_x(job + 1, 0)
                    if m == 1:
                        flip_x(job + 1, 1)

            njobs = pe.value_load(njobs_i[0:1, 0:1], min_val=E, max_val=JOBS_MAX - 2)
            with pe.Fori(0, njobs) as job:
                case = pe.value_load(jobs_i[0:1, 3, bass.ds(job, 1)], min_val=1, max_val=NCH * RING // HALF)
                pe.wait_ge(x_copied, job * 2 + 2)
                pe.wait_ge(gu_read, job * NCH + 1)

                def by_case(low, high):
                    if low == high:
                        run_job(job, (low - 1) % NCH + 1, (low - 1) // NCH * HALF)
                        return
                    middle = (low + high) // 2
                    with pe.If(case > middle):
                        by_case(middle + 1, high)
                    with pe.Else():
                        by_case(low, middle)

                by_case(1, NCH * RING // HALF)

        @block.scalar
        def _(act):
            act.sem_inc(t_copied, 1)
            act.dma_start(gain[:, :], norm1.partition_broadcast(P)).then_inc(gain_in, 16)
            act.wait_ge(eps_set, 1)
            act.activation(st[:, 17:18], eps, ACT.Sqrt).then_inc(table_in, 1)

            def square(src, n):
                act.activation(sq_junk, src, ACT.Square, accum_out=ssq[:, n % TT:n % TT + 1]).then_inc(ssq_done, 1)

            def root(n, k):
                act.activation(rstd[:, n % TT:n % TT + k], ssq[:, n % TT:n % TT + k], ACT.Sqrt,
                               bias=eps, scale=1.0 / D).then_inc(sqrt_done, k)

            for t in range(TT):
                act.wait_ge(x_in[t], 16)
                square(xs[:, t, :], t)
                act.wait_ge(ssq_done, t + 1)
                root(t, 1)
            for t in range(TT):
                act.wait_ge(tr_done, 2 * t + 1)
                act.activation(hT[:, 0:4, t * P:(t + 1) * P], bank[4][:, :].rearrange("p (k s) -> p k s", k=4),
                               ACT.Copy).then_inc(tr_act, 1)
            act.wait_ge(h_done, TT)
            act.dma_start(gain[:, :], norm2.partition_broadcast(P)).then_inc(gain_in, 16)

            copies = [0]

            def copy_group(dst, width, scale=1.0):
                n = copies[0]
                copies[0] += 1
                act.wait_ge(proj_done, n + 1)
                src = bank[n % 2][:, :]
                if width:
                    src = src.rearrange("p (t c) -> p t c", c=width)
                act.activation(dst, src, ACT.Copy, scale=scale).then_inc(proj_act, 1)

            def copy_q(pr):
                copy_group(qk[:, pr % 2, 0, :], 0, DH ** -0.5)

            def copy_k(pr):
                copy_group(qk[:, pr % 2, 1, :], 0)

            act.wait_ge(u_pad, 1)
            for m in range(2):
                copy_group(pa[:, m, 8:8 + S], 0)
            copy_q(0)
            copy_k(0)
            for i in range(3):
                for tp in range(2):
                    copy_group(v[:, 2 * tp:2 * tp + 2, i * 256:(i + 1) * 256], 256)
            for it in range(PAIRS + 1):
                for i in range(TT):
                    if it + 1 < PAIRS and i == 1:
                        copy_q(it + 1)
                    if it + 1 < PAIRS and i == 3:
                        copy_k(it + 1)
                    if it >= 1:
                        n = TT * (it - 1) + i
                        act.wait_ge(pt_done, n + 1)
                        a = tri(i) * P
                        act.activation(probT[:, 1, a:a + (i + 1) * P], bank[5][:, 0:(i + 1) * P], ACT.Copy)\
                            .then_inc(pt_act, 1)
                    if it < PAIRS:
                        n = TT * it + i
                        act.wait_ge(negmax_done, n + 1)
                        a = tri(i) * P
                        for h in range(2):
                            pv = prob[:, h, a:a + (i + 1) * P]
                            act.activation(pv, pv, ACT.Exp, bias=neg_max[:, h:h + 1],
                                           accum_out=row_sum[:, h:h + 1]).then_inc(exp_done, 1)
                if it == 0:
                    for m in range(2):
                        act.wait_ge(poolmm, m + 1)
                        act.activation(mixT[:, m, :], bank[7][:, :], ACT.Copy, scale=pscale[:, m:m + 1])\
                            .then_inc(pool_out, 1)
                if it >= 1:
                    act.wait_ge(pv_done, it)
                    act.activation(mixT[:, 1 + it, :], bank[6][:, :], ACT.Copy).then_inc(att_out, 1)

            def copy_h2(t):
                act.wait_ge(tr_done, 2 * (TT + t) + 1)
                act.activation(hT[:, 0:4, t * P:(t + 1) * P], bank[4][:, :].rearrange("p (k s) -> p k s", k=4),
                               ACT.Copy).then_inc(tr_act, 1)

            def sum_squares2(t):
                act.wait_ge(x2_done, t + 1)
                act.wait_ge(ssq_done, TT + t)
                square(xs[:, t, :], TT + t)
                act.wait_ge(ssq_done, TT + t + 1)
                root(TT + t, 1)

            sum_squares2(0)
            sum_squares2(1)
            copy_h2(0)
            sum_squares2(2)
            copy_h2(1)
            copy_h2(2)
            sum_squares2(3)
            copy_h2(3)
            act.wait_ge(gate_in, 1)
            act.activation(gates, gates, ACT.Exp).then_inc(gate_exp, 1)

            def copy_x(job, a):
                act.wait_ge(x_tr, job * 2 + (a + 1))
                act.activation(xT[:, 2 * a:2 * a + 2, :], bank[7][:, :].rearrange("p (c n) -> p c n", c=2),
                               ACT.Copy).then_inc(x_copied, 1)

            copy_x(0, 0)
            copy_x(0, 1)
            act.wait_ge(jobs_done, 2)
            njobs = act.value_load(njobs_i[0:1, 0:1], min_val=E, max_val=JOBS_MAX - 2)
            all_down = act.snap(njobs * NCH)
            with act.Fori(0, njobs) as job:
                act.wait_ge(y_done, job * NCH + 1)
                act.wait_ge(bias_mm, job * 2 + 1)
                act.activation(bt[:, 0:2 * Q], bank[7][:, 0:2 * Q], ACT.Copy).then_inc(bias_copied, 1)
                act.wait_ge(bias_mm, job * 2 + 2)
                act.activation(bt[:, 2 * Q:3 * Q], bank[7][:, 0:Q], ACT.Copy).then_inc(bias_copied, 1)

                def sigmoid(c):
                    act.wait_ge(gate_clamped, job * NCH + (c + 1))
                    act.activation(sg[:, c % 2, :], gu[:, c % 2, 0:Q], ACT.Sigmoid, scale=ALPHA)\
                        .then_inc(sig_done, 1)

                def copy_act(c):
                    act.wait_ge(t_done, job * NCH + (c + 2))
                    act.activation(aT[:, c, :], bank[6][:, 0:Q], ACT.Copy).then_inc(t_copied, 1)

                sigmoid(0)
                sigmoid(1)
                copy_act(0)
                sigmoid(2)
                copy_act(1)
                copy_x(job + 1, 0)
                sigmoid(3)
                copy_act(2)
                copy_x(job + 1, 1)
                copy_act(3)

            act.wait_ge(dn_done, all_down)
            act.dma_start(final_gain, final_g.partition_broadcast(P)).then_inc(gain_in, 16)
            for t in range(TT):
                act.wait_ge(sum_done, t + 1)
                act.wait_ge(ssq_done, 2 * TT + t)
                square(xs[:, t, :], 2 * TT + t)
                act.wait_ge(ssq_done, 2 * TT + t + 1)
                root(2 * TT + t, 1)

        @block.gpsimd
        def _(pool):
            steps = [0]

            def link(ins):
                ins.then_inc(pstep, 1)
                steps[0] += 1
                pool.wait_ge(pstep, steps[0])

            for c in range(NCH):
                pool.dma_start(ahead[0:16, 1, c, :], consts[0:16, 4 * c:4 * c + 4])\
                    .then_inc(scattered[c], 16)
            link(pool.memset(pb[:, :, 0:8], 0.0))
            link(pool.memset(pc[:, :, 0:8], 0.0))
            pool.memset(pa[:, :, 0:8], 0.0).then_inc(u_pad, 1)
            pool.wait_ge(r_copied, 2)
            pool.dma_start(bias_by_dist, r_sb).then_inc(r_out, 16)
            pool.wait_ge(r_out, 16)

            def load_table(pr):
                src = bass.AP(bias_by_dist.tensor, 2 * pr * RLEN, [[1, P], [RLEN, 2], [1, S]])
                pool.dma_start(btab[:, pr % 2, :, :], src).then_inc(bt_in[pr % 2], 16)

            load_table(0)
            load_table(1)
            pool.wait_ge(proj_act, 2)
            pool.wait_ge(u_pad, 1)
            pool.wait_ge(cst_in, 16)
            link(pool.tensor_tensor(pb[:, :, 8:8 + S], pa[:, :, 8:8 + S], pa[:, :, 7:7 + S], ALU.add))
            link(pool.tensor_tensor(pc[:, :, 8:8 + S], pb[:, :, 8:8 + S], pb[:, :, 6:6 + S], ALU.add))
            link(pool.tensor_tensor(pb[:, 1, 8:8 + S], pc[:, 1, 8:8 + S], pc[:, 1, 4:4 + S], ALU.add))
            link(pool.tensor_tensor(pc[PG:P, 1, 8:8 + S], pb[PG:P, 1, 8:8 + S], pb[PG:P, 1, 0:S], ALU.add))
            for m in range(2):
                for r, win in ((slice(0, PG), pb), (slice(PG, P), pc)):
                    ratio = cst[r, C_CNT + 16 * m:C_CNT + 16 * (m + 1)]
                    link(pool.tensor_tensor(win[r, m, 8:24], win[r, m, 8:24], ratio, ALU.mult))
                    link(pool.tensor_scalar(win[r, m, 8:8 + S], win[r, m, 8:8 + S],
                                            cst[r, C_INVW + m:C_INVW + m + 1], None, ALU.mult))
                    pool.tensor_tensor(pa[r, m, 8:8 + S], win[r, m, 8:8 + S], pa[r, m, 8:8 + S], ALU.subtract)\
                        .then_inc(pooled, 1)
            pool.wait_ge(pooled, 4)
            for pr in range(PAIRS):
                for i in range(TT):
                    n = TT * pr + i
                    pool.wait_ge(inv_done, n + 1)
                    a = tri(i) * P
                    for h in range(2):
                        pv = prob[:, h, a:a + (i + 1) * P]
                        pool.tensor_scalar(pv, pv, row_inv[:, h:h + 1], None, ALU.mult).then_inc(norm_done, 1)
                if pr + 2 < PAIRS:
                    pool.wait_ge(score_read, TT * (pr + 1))
                    load_table(pr + 2)
            h2v = h2_rows.rearrange("(t p r) q -> t p (r q)", t=TT, p=P)
            for t in range(TT):
                pool.wait_ge(h_done, TT + t + 1)
                pool.dma_start(h2v[t], hbuf[:, t % 2, :]).then_inc(h2_out[t % 2], 16)
            for b in range(2):
                pool.wait_ge(h2_out[b], 16 * TT // 2)

            last_token, last_row = pool.to_reg(S * 4 - 1), pool.to_reg(S * TOPK * 4 - 1)

            def signal(c, done, b):
                pool.dma_start(ahead[0:16, b, c, :], consts[0:16, 4 * c:4 * c + 4]).then_inc(done, 16)

            def gather_chunk(c):
                pool.indirect_dma_start(xg[:, c, :], None, h2_rows,
                                        bass.IndirectOffsetOnAxis(ap=idx_g[:, c:c + 1], axis=0),
                                        bounds_check=last_token, oob_is_err=False).then_inc(gathered[c], 16)

            def gather(chunks):
                gather_chunk(0)
                for c in range(1, NCH):
                    with pool.If(chunks > c):
                        gather_chunk(c)
                    with pool.If(chunks <= c):
                        signal(c, gathered[c], 0)

            def scatter_chunk(c):
                pool.indirect_dma_start(y_rows, bass.IndirectOffsetOnAxis(ap=idx_s[:, c:c + 1], axis=0),
                                        yb[:, c, :], None, bounds_check=last_row, oob_is_err=False)\
                    .then_inc(scattered[c], 16)

            pool.wait_ge(lg_done, TT)
            pool.wait_ge(tr_done, 4 * TT)
            pool.memset(xg, 0.0).then_inc(xg_zero, 1)
            pool.wait_ge(xg_zero, 1)
            pool.wait_ge(idx_done, 1)
            for c in range(NCH):
                gather_chunk(c)
            pool.wait_ge(jobs_done, 2)
            njobs = pool.value_load(njobs_i[0:1, 0:1], min_val=E, max_val=JOBS_MAX - 2)
            with pool.Fori(0, njobs) as job:
                chunks = pool.value_load(jobs_i[0:1, 2, bass.ds(job, 1)], min_val=1, max_val=NCH)
                next_chunks = pool.value_load(jobs_i[0:1, 2, bass.ds(job + 1, 1)], min_val=1, max_val=NCH)
                pool.wait_ge(idx_done, job + 2)
                pool.wait_ge(x_tr, job * 2 + 2)
                pool.sem_inc(waited_pool, 1)
                gather(next_chunks)
                for c in range(NCH):
                    pool.wait_ge(y_done, job * NCH + (c + 2))
                    pool.sem_inc(waited_pool, 1)
                    if c == 0:
                        scatter_chunk(c)
                        continue
                    with pool.If(chunks > c):
                        scatter_chunk(c)
                    with pool.If(chunks <= c):
                        signal(c, scattered[c], 1)
            for c in range(NCH):
                pool.wait_ge(gathered[c], njobs * 16 + 16)

        @block.vector
        def _(dve):
            steps = [0]

            def link(ins):
                ins.then_inc(step, 1)
                steps[0] += 1
                dve.wait_ge(step, steps[0])

            dve.sem_inc(gu_read, 1)
            dve.sem_inc(y_done, 1)
            dve.memset(eps, EPS).then_inc(eps_set, 1)
            dve.memset(relb[BUCKETS:BUCKETS + 1, :], 1.0).then_inc(relb_one, 1)

            def norm(t, phase):
                if t >= 2 or phase:
                    dve.wait_ge(tr_done, 2 * (phase * TT + t - 1))
                if phase and t >= 2:
                    dve.wait_ge(h2_out[t % 2], 16 * (t // 2))
                dve.scalar_tensor_tensor(hbuf[:, t % 2, :], xs[:, t, :], rstd[:, t:t + 1], gain[:, :],
                                         ALU.mult, ALU.mult).then_inc(h_done, 1)

            def copy_h(t, phase):
                dve.wait_ge(tr_done, 2 * (phase * TT + t + 1))
                dve.tensor_copy(hT[:, 4:8, t * P:(t + 1) * P], bank[5][:, :].rearrange("p (k s) -> p k s", k=4))\
                    .then_inc(tr_dve, 1)

            dve.wait_ge(gain_in, 16)
            for t in range(TT + 1):
                if t < TT:
                    dve.wait_ge(sqrt_done, t + 1)
                    link(dve.reciprocal(rstd[:, t:t + 1], rstd[:, t:t + 1]))
                    norm(t, 0)
                if t >= 1:
                    copy_h(t - 1, 0)
            dve.wait_ge(r_mm, 1)
            for a in range(2):
                dve.tensor_copy(r_sb[:, a * RLEN // 2:(a + 1) * RLEN // 2], bank[2 + a][0:HEADS, 0:RLEN // 2])\
                    .then_inc(r_copied, 1)

            def invert(n):
                dve.wait_ge(exp_done, 2 * (n + 1))
                if n:
                    dve.wait_ge(norm_done, 2 * n)
                dve.reciprocal(row_inv, row_sum).then_inc(inv_done, 1)

            for it in range(PAIRS + 1):
                for i in range(TT):
                    n = TT * it + i
                    if 0 < n <= TT * PAIRS:
                        invert(n - 1)
                    if it >= 1:
                        dve.wait_ge(pt_done, TT * (it - 1) + i + 1)
                        a = tri(i) * P
                        dve.tensor_copy(probT[:, 0, a:a + (i + 1) * P], bank[4][:, 0:(i + 1) * P])\
                            .then_inc(pt_dve, 1)
                    if it < PAIRS:
                        dve.wait_ge(score_done, n + 1)
                        if i == 0:
                            dve.wait_ge(bt_in[it % 2], 16 * (it // 2 + 1))
                        a = tri(i) * P
                        for h in range(2):
                            ins = dve.tensor_tensor_reduce(prob[:, h, a:a + (i + 1) * P], bank[2 + h][:, 0:(i + 1) * P],
                                                           btab[:, it % 2, h, 0:(i + 1) * P][:, ::-1], 1.0, -3e38,
                                                           ALU.add, ALU.max, row_max[:, h:h + 1])
                        ins.then_inc(score_read, 1)
                        dve.wait_ge(score_read, n + 1)
                        dve.tensor_scalar(neg_max, row_max, -1.0, None, ALU.mult).then_inc(negmax_done, 1)

            iota = cst[:, C_IOTA:C_IOTA + E]
            tok = cst[:, C_TOK:C_TOK + TT * TOPK].rearrange("p (t k) -> p t k", t=TT)
            for c in range(NCH):
                link(dve.tensor_scalar(slot.rearrange("p (c j s) -> p c j s", c=NCH, j=4)[:, c],
                                       iota.unsqueeze(1).broadcast_to([P, 4, CH]), float(c * CH), None, ALU.add))
            dve.tensor_copy(tri16, tri_c)
            link(dve.tensor_copy(ones16, ones))
            link(dve.tensor_copy(pcol[:, :, 0], cst[:, C_TOK4:C_TOK4 + TT]))
            link(dve.tensor_scalar(pcol[:, :, 2], cst[:, C_TOK4:C_TOK4 + TT], 0.0, 1.0, ALU.mult, ALU.add))
            def residual(t):
                dve.wait_ge(op_done, t + 1)
                for n in range(2):
                    part = xs[:, t, n * 512:(n + 1) * 512]
                    ins = dve.tensor_tensor(part, bank[2 * (t % 2) + n][:, :], part, ALU.add)
                    if n == 1:
                        ins.then_inc(x2_done, 1)

            def norm2(t):
                dve.wait_ge(sqrt_done, TT + t + 1)
                link(dve.reciprocal(rstd[:, t:t + 1], rstd[:, t:t + 1]))
                if t == 0:
                    dve.wait_ge(gain_in, 32)
                norm(t, 1)

            def choose(t):
                dve.wait_ge(lg_done, t + 1)
                dve.tensor_copy(logits[:, t, :], bank[6][:, t * E:(t + 1) * E]).then_inc(lg_copied, 1)
                dve.wait_ge(lg_copied, t + 1)
                link(dve.max(top[:, t, :], logits[:, t, :]))
                link(dve.max_index(topi[:, t, :], top[:, t, :], logits[:, t, :]))
                link(dve.tensor_copy(topf[:, t, :], topi[:, t, :]))
                shape = [P, TOPK, E]
                link(dve.tensor_tensor(chose[:, t], iota.unsqueeze(1).broadcast_to(shape),
                                       topf[:, t, 0:TOPK].unsqueeze(2).broadcast_to(shape), ALU.is_equal))
                by_expert = chose[:, t].rearrange("p k e -> p e k")
                with nc.allow_low_precision(reason="sums of one 1 at the most"):
                    dve.tensor_reduce(mask[:, t, :], by_expert, AX.X, ALU.add).then_inc(mask_done, 1)
                dve.wait_ge(mask_done, t + 1)
                link(dve.tensor_tensor(chose[:, t], chose[:, t], tok[:, t, :].unsqueeze(2).broadcast_to(shape),
                                       ALU.mult))
                link(dve.tensor_reduce(pos4[:, t, :], by_expert, AX.X, ALU.add))

            def job_columns(e, n, wait):
                wait(dve.tensor_scalar(job_r, rank[:, :, bass.ds(e, 1)].rearrange("p t e -> p (t e)"),
                                       jobs_f[:, 1, bass.ds(n, 1)] if n is not None else 0.0, float(FAR),
                                       ALU.subtract, ALU.add))
                dve.tensor_copy(pcol[:, :, 1], pos4[:, :, bass.ds(e, 1)].rearrange("p t e -> p (t e)"))
                for t in range(TT):
                    ins = dve.tensor_scalar(hot[:, t, :], slot, job_r[:, t:t + 1], None, ALU.is_equal)
                ins.then_inc(hot_done, 1)

            def job_picker(e):
                dve.tensor_copy(pick.rearrange("p (j s) -> p j s", j=4),
                                ident[:, bass.ds(e * 4, 4)].unsqueeze(2).broadcast_to([P, 4, CH]))\
                    .then_inc(pick_done, 1)

            def job_rows(n, wait):
                dve.wait_ge(idx_mm, n + 1)
                rows = bank[7][:, 0:4 * NCH].rearrange("p (c n) -> p c n", c=NCH)
                wait(dve.tensor_copy(job_p.unsqueeze(2), rows[:, :, 2:3]))
                wait(dve.scalar_tensor_tensor(idx_t, job_p.unsqueeze(2).broadcast_to([P, NCH, 2]), float(-SKIP),
                                              rows[:, :, 0:2],
                                              ALU.mult, ALU.add))
                dve.tensor_scalar(idx_g, idx_t[:, :, 0], cst[:, C_SKIPJ:C_SKIPJ + 1], None, ALU.add)\
                    .then_inc(idx_done, 1)

            residual(0)
            norm2(0)
            residual(1)
            norm2(1)
            copy_h(0, 1)
            residual(2)
            norm2(2)
            choose(0)
            copy_h(1, 1)
            choose(1)
            copy_h(2, 1)
            residual(3)
            norm2(3)
            choose(2)
            copy_h(3, 1)
            choose(3)
            dve.wait_ge(rank_mm, 1)
            link(dve.scalar_tensor_tensor(rank, mask, float(-FAR),
                                          bank[0][:, 0:TT * E].rearrange("p (t e) -> p t e", t=TT),
                                          ALU.mult, ALU.add))
            job_columns(0, None, link)
            job_rows(0, link)
            dve.wait_ge(cnt_mm, 1)
            link(dve.tensor_copy(cnt, bank[1][:, 0:E]))
            link(dve.tensor_scalar(nblk, cnt, float(P), None, ALU.is_gt))
            for b in range(2, TT):
                link(dve.scalar_tensor_tensor(nblk, cnt, float(b * P), nblk, ALU.is_gt, ALU.add))
            link(dve.tensor_tensor_scan(blk_end, ones[:, 0:E], nblk, float(E), ALU.mult, ALU.add))
            part = cst[:, C_PART:C_PART + 1]
            link(dve.tensor_scalar(before, blk_end, part, 0.0, ALU.is_le, ALU.add, accum_out=jcol[:, 0:1]))
            link(dve.tensor_tensor_reduce(tmp32, before, nblk, 1.0, 0.0, ALU.mult, ALU.add, jcol[:, 1:2]))
            link(dve.tensor_scalar(jcol[:, 0:1], jcol[:, 0:1], float(E - 1), cst[:, C_FIRST:C_FIRST + 1],
                                   ALU.min, ALU.add))
            link(dve.tensor_scalar(tmp32, iota, jcol[:, 0:1], None, ALU.is_equal))
            link(dve.tensor_tensor_reduce(tmp32, tmp32, cnt, 1.0, 0.0, ALU.mult, ALU.add, jcol[:, 2:3]))
            link(dve.tensor_scalar(jcol[:, 3:4], jcol[:, 1:2], part, float(-P), ALU.subtract, ALU.mult))
            link(dve.tensor_scalar(jcol[:, 3:4], jcol[:, 3:4], float(-P * (E - 1)), 0.0, ALU.add, ALU.max))
            link(dve.tensor_tensor(jcol[:, 4:5], jcol[:, 2:3], jcol[:, 3:4], ALU.subtract))
            link(dve.tensor_scalar(jcol[:, 5:6], jcol[:, 4:5], float(CH), 1.0, ALU.is_gt, ALU.add))
            for c in range(2, NCH):
                link(dve.scalar_tensor_tensor(jcol[:, 5:6], jcol[:, 4:5], float(c * CH), jcol[:, 5:6],
                                              ALU.is_gt, ALU.add))
            link(dve.tensor_tensor(jcol[:, 6:7], jcol[:, 5:6], cst[:, C_PHASE:C_PHASE + 1], ALU.add))
            for n, col in enumerate((0, 3, 5, 6)):
                ins = dve.tensor_scalar(jdiag[:, n * JOBS_MAX:(n + 1) * JOBS_MAX], ident[:, 0:JOBS_MAX],
                                        jcol[:, col:col + 1], None, ALU.mult)
            ins.then_inc(jdiag_done, 1)
            dve.wait_ge(jobs_mm, 1)
            table = bank[1][:, 0:4 * JOBS_MAX].rearrange("p (r n) -> p r n", r=4)
            link(dve.tensor_copy(jobs_f[:, :, :], table))
            dve.tensor_copy(njobs_i[:, :], blk_end[:, E - 1:E]).then_inc(jobs_done, 1)
            dve.tensor_copy(jobs_i[:, :, :], jobs_f[:, :, :]).then_inc(jobs_done, 1)
            gv = gates.rearrange("p (t k) -> p t k", t=TT)
            dve.tensor_tensor(gv, top[:, :, 0:TOPK], top[:, :, 0:1].broadcast_to([P, TT, TOPK]), ALU.subtract)\
                .then_inc(gate_in, 1)

            job_columns(1, None, link)
            job_picker(0)
            link(dve.tensor_copy(keep_s, idx_t[:, :, 1]))
            njobs = dve.value_load(njobs_i[0:1, 0:1], min_val=E, max_val=JOBS_MAX - 2)
            base = steps[0]
            with dve.Fori(0, njobs) as job:
                inner = [0]

                def link_job(ins):
                    ins.then_inc(step, 1)
                    inner[0] += 1
                    dve.wait_ge(step, job * STEPS + (base + inner[0]))

                e = dve.value_load(jobs_i[0:1, 0, bass.ds(job + 1, 1)], min_val=0, max_val=E - 1)
                after = dve.value_load(jobs_i[0:1, 0, bass.ds(job + 2, 1)], min_val=0, max_val=E - 1)
                job_rows(job + 1, link_job)
                dve.wait_ge(bias_copied, job * 2 + 2)
                for c in range(NCH):
                    b = c % 2
                    gate, up = gu[:, b, 0:Q], gu[:, b, Q:2 * Q]
                    dve.wait_ge(gu_done, job * NCH + (c + 1))
                    dve.tensor_tensor(gu[:, b, :], bank[c][:, :], bt[:, 0:2 * Q], ALU.add).then_inc(gu_read, 1)
                    dve.wait_ge(gu_read, job * NCH + (c + 2))
                    dve.tensor_scalar(gate, gate, LIMIT, None, ALU.min).then_inc(gate_clamped, 1)
                    link_job(dve.tensor_scalar(up, up, LIMIT, -LIMIT, ALU.min, ALU.max))
                    dve.wait_ge(gate_clamped, job * NCH + (c + 1))
                    link_job(dve.scalar_tensor_tensor(up, up, 1.0, gate, ALU.add, ALU.mult))
                    dve.wait_ge(t_done, job * NCH + max(c, 1))
                    dve.wait_ge(sig_done, job * NCH + (c + 1))
                    dve.tensor_tensor(act_q[b], up, sg[:, b, :], ALU.mult).then_inc(act_done, 1)
                job_picker(e)
                job_columns(after, job + 2, link_job)
                for c in range(NCH):
                    dve.wait_ge(scattered[c], job * 16 + 16)
                link_job(dve.tensor_scalar(idx_s, keep_s, cst[:, C_SKIPJ:C_SKIPJ + 1], None, ALU.add))
                link_job(dve.tensor_copy(keep_s, idx_t[:, :, 1]))
                for c in range(NCH):
                    dve.wait_ge(dn_done, job * NCH + (c + 1))
                    dve.tensor_tensor(yb[:, c, :], bank[4 + c % 2][:, 0:Q], bt[:, 2 * Q:3 * Q], ALU.add)\
                        .then_inc(y_done, 1)
                assert inner[0] == STEPS

            dve.wait_ge(gate_exp, 1)
            total = [0]

            def link_end(ins):
                ins.then_inc(step, 1)
                total[0] += 1
                dve.wait_ge(step, njobs * STEPS + (base + total[0]))

            link_end(dve.tensor_reduce(gsum, gv, AX.X, ALU.add))
            link_end(dve.reciprocal(ginv, gsum))
            link_end(dve.tensor_tensor(gv, gv, ginv.unsqueeze(2).broadcast_to([P, TT, TOPK]), ALU.mult))
            dve.wait_ge(gain_in, 48)

            def add_experts(t):
                rows = ring[:, 3 * t:3 * t + 2, :].rearrange("p a (k d) -> p (a k) d", k=2)
                for k in range(TOPK):
                    if k % 2 == 0:
                        dve.wait_ge(y_in[t][k // 2], 16)
                    ins = dve.scalar_tensor_tensor(xs[:, t, :], rows[:, k, :], gv[:, t, k:k + 1], xs[:, t, :],
                                                   ALU.mult, ALU.add)
                    if k < TOPK - 1:
                        link_end(ins)
                ins.then_inc(sum_done, 1)

            def final_norm(t):
                dve.wait_ge(sqrt_done, 2 * TT + t + 1)
                link_end(dve.reciprocal(rstd[:, t:t + 1], rstd[:, t:t + 1]))
                for a in range(2):
                    c = slice(a * D // 2, (a + 1) * D // 2)
                    dve.scalar_tensor_tensor(ring[:, 3 * t + 2, c], xs[:, t, c], rstd[:, t:t + 1], final_gain[:, c],
                                             ALU.mult, ALU.mult).then_inc(fin_done, 1)

            for t in range(TT):
                add_experts(t)
                if t >= 1:
                    final_norm(t - 1)
            final_norm(TT - 1)


STEPS = 5 + 2 * NCH


def kernel(x, norm1_g, w_in, pool_w, pool_scale, rel_bias, w_out, norm2_g, router_w, router_b,
           w_gate_up, b_gate_up, w_down, b_down, final_g):
    import concourse.bacc as bacc
    from concourse.bass_utils import run_bass_kernel_spmd

    def a(t):
        return np.ascontiguousarray(np.asarray(t))

    wi = a(w_in)[0]
    q0, k0, v0 = POOL_W, POOL_W + ATT_W, POOL_W + 2 * ATT_W
    pair = [np.concatenate([wi[:, q0 + P * i:q0 + P * (i + 1)], wi[:, k0 + P * i:k0 + P * (i + 1)]], 1)
            for i in range(PAIRS)]
    units = [wi[:, 0:POOL_W], pair[0]] + [wi[:, v0 + 256 * i:v0 + 256 * (i + 1)] for i in range(3)] + pair[1:]
    units = np.stack([u.reshape(KT, P, 256).transpose(1, 0, 2).reshape(P, UNIT) for u in units])
    biases = np.concatenate([a(b_gate_up)[0].reshape(E, 2, 4, Q).transpose(0, 2, 1, 3).reshape(E * 4, 2 * Q),
                             a(b_down)[0].reshape(E * 4, Q)], 1)
    cst, sel = constants()
    ins = {
        "x": a(x)[0], "w_in": units, "w_out": a(w_out)[0],
        "norm1": a(norm1_g)[0], "norm2": a(norm2_g)[0], "final_g": a(final_g),
        "rel_bias": a(rel_bias),
        "pool_w": a(pool_w)[0].reshape(2, 2, PG, PG).transpose(1, 2, 0, 3).reshape(P, 2, PG),
        "pool_scale": a(pool_scale)[0].reshape(2, P).T,
        "router_w": a(router_w)[0].reshape(KT, P, E).transpose(1, 0, 2), "router_b": a(router_b),
        "w_gate_up": a(w_gate_up)[0], "w_down": a(w_down)[0], "biases": biases,
        "consts": cst, "selector": sel,
        "turn_table": (np.arange(2 * JOBS_MAX, dtype=np.int32) * HALF % RING)[None, :],
    }
    nc = bacc.Bacc("TRN2", target_bir_lowering=False, num_devices=1)
    arrays, args = {}, []
    for name, t in ins.items():
        t = np.ascontiguousarray(t)
        arrays[f"in_{name}"] = t
        args.append(nc.dram_tensor(f"in_{name}", t.shape, mybir.dt.from_np(t.dtype), kind="ExternalInput").ap())
    out = nc.dram_tensor("out_0", (S, D), F32, kind="ExternalOutput").ap()
    program(nc, *args, out)
    r = run_bass_kernel_spmd(nc, [arrays], core_ids=[0])
    return r.results[0]["out_0"].reshape(1, S, D)
```
